# Optimizing a Trainium2 kernel written in Bass

```python
import math
import jax
import jax.numpy as jnp
from jax import lax
import numpy as np
import jax, jax.numpy as jnp

D_MODEL = 1024
BATCH = 1
SEQ = 512
DEPTH = 1

GRID_W = 64
CTX_LEN = 256

DN_HEADS = 4
DN_DK = 128
DN_DV = 128
DN_QK = DN_HEADS * DN_DK
DN_WIDTH = DN_HEADS * DN_DV
DN_CONV_DIM = 2 * DN_QK + DN_WIDTH
SHORT_CONV = 7
CHUNK = 64

CF_CH = 512
CF_K = 31

D_MIX = DN_WIDTH + CF_CH
OFF_Z = DN_CONV_DIM
OFF_BA = OFF_Z + DN_WIDTH
OFF_CF = OFF_BA + 4 * DN_HEADS
D_IN = OFF_CF + 2 * CF_CH

N_EXPERTS = 64
TOP_K = 6
N_GROUPS = 8
TOPK_GROUPS = 4
D_EXPERT = 256
D_SHARED = 256
ROUTED_SCALE = 2.5
MOE_BLOCK = 128

EPS = 1e-6


def rmsnorm(x, g):
    xf = x.astype(jnp.float32)
    y = xf * lax.rsqrt(jnp.mean(xf * xf, axis=-1, keepdims=True) + EPS)
    return (y * g.astype(jnp.float32)).astype(x.dtype)

def layernorm(x, g, b):
    xf = x.astype(jnp.float32)
    mu = jnp.mean(xf, axis=-1, keepdims=True)
    var = jnp.mean(jnp.square(xf - mu), axis=-1, keepdims=True)
    y = (xf - mu) * lax.rsqrt(var + EPS) * g.astype(jnp.float32) + b.astype(jnp.float32)
    return y.astype(x.dtype)

def l2norm(x):
    return x * lax.rsqrt(jnp.sum(x * x, axis=-1, keepdims=True) + EPS)

def modulate(h, shift, scale):
    return h * (1 + scale) + shift

def depthwise_conv_seq(x, w):
    k, ch = w.shape
    return lax.conv_general_dilated(x, w[:, None, :].astype(x.dtype), (1,), [(k // 2, k // 2)],
                                    dimension_numbers=('NWC', 'WIO', 'NWC'), feature_group_count=ch)

def depthwise_conv_grid_columns(x, w):
    bsz, n, ch = x.shape
    rows = n // GRID_W
    k = w.shape[0]
    y = lax.conv_general_dilated(x.reshape(bsz, rows, GRID_W, ch), w[:, None, None, :].astype(x.dtype),
                                 (1, 1), [(k // 2, k // 2), (0, 0)],
                                 dimension_numbers=('NHWC', 'HWIO', 'NHWC'), feature_group_count=ch)
    return y.reshape(bsz, n, ch)

def split_mixer_inputs(u):
    return u[..., :OFF_Z], u[..., OFF_Z:OFF_BA], u[..., OFF_BA:OFF_CF], u[..., OFF_CF:]

def delta_inputs(qkv, ba, conv_w, a_log, dt_bias):
    bsz, n, _ = qkv.shape
    qkv = jax.nn.silu(depthwise_conv_seq(qkv, conv_w)).astype(jnp.float32)
    q = l2norm(qkv[..., :DN_QK].reshape(bsz, n, DN_HEADS, DN_DK)) * (DN_DK ** -0.5)
    k = l2norm(qkv[..., DN_QK:2 * DN_QK].reshape(bsz, n, DN_HEADS, DN_DK))
    v = qkv[..., 2 * DN_QK:].reshape(bsz, n, DN_HEADS, DN_DV)
    ba = ba.astype(jnp.float32).reshape(bsz, n, 2, 2, DN_HEADS)
    beta = jax.nn.sigmoid(ba[:, :, :, 0])
    g = -jnp.exp(a_log.astype(jnp.float32)) * jax.nn.softplus(ba[:, :, :, 1] + dt_bias.astype(jnp.float32))
    return q, k, v, beta, g

def gated_delta_chunked(q, k, v, g, beta, s0):
    bsz, n, heads, dk = q.shape
    dv = v.shape[-1]
    nc = n // CHUNK

    def blocks(t):
        t = t.reshape(bsz, nc, CHUNK, heads, *t.shape[3:])
        return jnp.moveaxis(t, (1, 3), (0, 2))

    qc, kc, vc, bc = blocks(q), blocks(k), blocks(v), blocks(beta)
    gc = jnp.cumsum(blocks(g), axis=-1)
    tri_incl = jnp.tril(jnp.ones((CHUNK, CHUNK), dtype=bool))
    tri_strict = jnp.tril(jnp.ones((CHUNK, CHUNK), dtype=bool), -1)
    decay = jnp.exp(jnp.where(tri_incl, gc[..., :, None] - gc[..., None, :], -jnp.inf))
    kb = kc * bc[..., None]
    lmat = jnp.where(tri_strict, jnp.einsum('nbhik,nbhjk->nbhij', kb, kc) * decay, 0.0)
    eye = jnp.eye(CHUNK, dtype=lmat.dtype)
    tinv = lax.linalg.triangular_solve(eye + lmat, jnp.broadcast_to(eye, lmat.shape),
                                       left_side=True, lower=True, unit_diagonal=True)
    u = jnp.einsum('nbhij,nbhjv->nbhiv', tinv, vc * bc[..., None])
    w = jnp.einsum('nbhij,nbhjk->nbhik', tinv, kb * jnp.exp(gc)[..., None])
    intra = jnp.einsum('nbhik,nbhjk->nbhij', qc, kc) * decay
    qd = qc * jnp.exp(gc)[..., None]
    kd = kc * jnp.exp(gc[..., -1:] - gc)[..., None]
    glast = jnp.exp(gc[..., -1])

    def step(s, inp):
        u_i, w_i, a_i, qd_i, kd_i, gl_i = inp
        v_new = u_i - jnp.einsum('bhck,bhkv->bhcv', w_i, s)
        o = jnp.einsum('bhck,bhkv->bhcv', qd_i, s) + jnp.einsum('bhij,bhjv->bhiv', a_i, v_new)
        s = s * gl_i[..., None, None] + jnp.einsum('bhck,bhcv->bhkv', kd_i, v_new)
        return s, o

    s_fin, o = lax.scan(step, s0, (u, w, intra, qd, kd, glast))
    o = jnp.moveaxis(o, (0, 2), (1, 3)).reshape(bsz, n, heads, dv)
    return o, s_fin

def bidir_gated_delta(q, k, v, beta, g, s0_fwd, s0_bwd):
    o_f, s_f = gated_delta_chunked(q, k, v, g[:, :, 0], beta[:, :, 0], s0_fwd)
    fl = lambda t: jnp.flip(t, axis=1)
    o_b, s_b = gated_delta_chunked(fl(q), fl(k), fl(v), fl(g[:, :, 1]), fl(beta[:, :, 1]), s0_bwd)
    return o_f + fl(o_b), s_f, s_b

def gated_head_norm(o, z, norm_g):
    bsz, n = z.shape[0], z.shape[1]
    on = o * lax.rsqrt(jnp.mean(o * o, axis=-1, keepdims=True) + EPS) * norm_g.astype(jnp.float32)
    gate = jax.nn.silu(z.astype(jnp.float32)).reshape(bsz, n, DN_HEADS, DN_DV)
    return (on * gate).reshape(bsz, n, DN_WIDTH).astype(z.dtype)

def conformer_module(cf_in, conv_fn, dw_w, dw_b, ln_g, ln_b):
    y = cf_in[..., :CF_CH] * jax.nn.sigmoid(cf_in[..., CF_CH:])
    y = conv_fn(y, dw_w) + dw_b
    return jax.nn.silu(layernorm(y, ln_g, ln_b))

def swiglu(h, wg, wu, wd):
    return (jax.nn.silu(h @ wg) * (h @ wu)) @ wd

def moe_ffn(h, router_w, router_bias, w_gate, w_up, w_down, s_gate, s_up, s_down):
    bsz, n, d = h.shape
    t = bsz * n
    hf = h.reshape(t, d)
    scores = jax.nn.sigmoid((hf @ router_w).astype(jnp.float32))
    sel = scores + router_bias.astype(jnp.float32)
    grp_score = lax.top_k(sel.reshape(t, N_GROUPS, N_EXPERTS // N_GROUPS), 2)[0].sum(-1)
    _, grp_idx = lax.top_k(grp_score, TOPK_GROUPS)
    grp_keep = jnp.any(grp_idx[..., None] == jnp.arange(N_GROUPS), axis=-2)
    exp_keep = jnp.repeat(grp_keep, N_EXPERTS // N_GROUPS, axis=-1)
    _, top_idx = lax.top_k(jnp.where(exp_keep, sel, -jnp.inf), TOP_K)
    top_w = jnp.take_along_axis(scores, top_idx, axis=-1)
    top_w = top_w / jnp.sum(top_w, axis=-1, keepdims=True) * ROUTED_SCALE
    tk = t * TOP_K
    flat_e = top_idx.reshape(tk)
    order = jnp.argsort(flat_e, stable=True)
    sorted_e = flat_e[order]
    sorted_tok = (order // TOP_K).astype(jnp.int32)
    sorted_w = top_w.reshape(tk)[order]
    counts = jnp.bincount(flat_e, length=N_EXPERTS)
    padded = (counts + MOE_BLOCK - 1) // MOE_BLOCK * MOE_BLOCK
    start = jnp.cumsum(counts) - counts
    pad_end = jnp.cumsum(padded)
    pad_start = pad_end - padded
    dest = pad_start[sorted_e] + jnp.arange(tk) - start[sorted_e]
    n_blocks = -(-tk // MOE_BLOCK) + N_EXPERTS
    n_slots = n_blocks * MOE_BLOCK
    slot_tok = jnp.full((n_slots,), t, jnp.int32).at[dest].set(sorted_tok)
    slot_w = jnp.zeros((n_slots,), jnp.float32).at[dest].set(sorted_w)
    block_exp = jnp.minimum(jnp.searchsorted(pad_end, jnp.arange(n_blocks) * MOE_BLOCK, side='right'),
                            N_EXPERTS - 1)
    h_pad = jnp.concatenate([hf, jnp.zeros((1, d), hf.dtype)], axis=0)

    def expert_block(args):
        tok, e = args
        return swiglu(h_pad[tok], w_gate[e], w_up[e], w_down[e])

    out = lax.map(expert_block, (slot_tok.reshape(n_blocks, MOE_BLOCK), block_exp))
    weighted = (out.reshape(n_slots, d) * slot_w[:, None]).astype(h.dtype)
    routed = jnp.zeros((t + 1, d), h.dtype).at[slot_tok].add(weighted)[:t]
    return (routed + swiglu(hf, s_gate, s_up, s_down)).reshape(bsz, n, d)

def first_inputs(seed: int = 0) -> dict:
    key = jax.random.key(seed)
    ks = jax.random.split(key, 32)
    f32 = jnp.float32
    L = DEPTH

    def nrm(k, shape, s):
        return jax.random.normal(k, shape, f32) * s

    dt = jnp.exp(jax.random.uniform(ks[11], (L, 2, DN_HEADS), f32, math.log(1e-3), math.log(1e-1)))
    return {
        'x': nrm(ks[0], (BATCH, SEQ, D_MODEL), 1.0),
        'c': nrm(ks[1], (BATCH, D_MODEL), 1.0),
        'ctx': nrm(ks[2], (BATCH, CTX_LEN, D_MODEL), 1.0),
        'c_ctx': nrm(ks[3], (D_MODEL,), 1.0),
        'w_mod': nrm(ks[4], (L, D_MODEL, 6 * D_MODEL), 0.5 * D_MODEL ** -0.5),
        'b_mod': nrm(ks[5], (L, 6 * D_MODEL), 0.02),
        'g_mix': 1.0 + nrm(ks[6], (L, D_MODEL), 0.02),
        'g_ffn': 1.0 + nrm(ks[7], (L, D_MODEL), 0.02),
        'w_in': nrm(ks[8], (L, D_MODEL, D_IN), D_MODEL ** -0.5),
        'w_out': nrm(ks[9], (L, D_MIX, D_MODEL), D_MIX ** -0.5),
        'dn_conv_w': nrm(ks[10], (L, SHORT_CONV, DN_CONV_DIM), SHORT_CONV ** -0.5),
        'dn_a_log': jnp.log(jax.random.uniform(ks[12], (L, 2, DN_HEADS), f32, 1.0, 16.0)),
        'dn_dt_bias': dt + jnp.log(-jnp.expm1(-dt)),
        'dn_norm_g': 1.0 + nrm(ks[13], (L, DN_DV), 0.02),
        'cf_dw_w': nrm(ks[14], (L, CF_K, CF_CH), CF_K ** -0.5),
        'cf_dw_b': nrm(ks[15], (L, CF_CH), 0.02),
        'cf_ln_g': 1.0 + nrm(ks[16], (L, CF_CH), 0.02),
        'cf_ln_b': nrm(ks[17], (L, CF_CH), 0.02),
        'router_w': nrm(ks[18], (L, D_MODEL, N_EXPERTS), D_MODEL ** -0.5),
        'router_bias': nrm(ks[19], (L, N_EXPERTS), 0.01),
        'exp_w_gate': nrm(ks[20], (L, N_EXPERTS, D_MODEL, D_EXPERT), D_MODEL ** -0.5),
        'exp_w_up': nrm(ks[21], (L, N_EXPERTS, D_MODEL, D_EXPERT), D_MODEL ** -0.5),
        'exp_w_down': nrm(ks[22], (L, N_EXPERTS, D_EXPERT, D_MODEL), D_EXPERT ** -0.5),
        'sh_w_gate': nrm(ks[23], (L, D_MODEL, D_SHARED), D_MODEL ** -0.5),
        'sh_w_up': nrm(ks[24], (L, D_MODEL, D_SHARED), D_MODEL ** -0.5),
        'sh_w_down': nrm(ks[25], (L, D_SHARED, D_MODEL), D_SHARED ** -0.5),
        'g_final': 1.0 + nrm(ks[26], (D_MODEL,), 0.02),
    }

def first_block(x, c, ctx, c_ctx, w_mod, b_mod, g_mix, g_ffn, w_in, w_out, dn_conv_w, dn_a_log, dn_dt_bias,
              dn_norm_g, cf_dw_w, cf_dw_b, cf_ln_g, cf_ln_b, router_w, router_bias, exp_w_gate, exp_w_up,
              exp_w_down, sh_w_gate, sh_w_up, sh_w_down, g_final):
    bsz = x.shape[0]
    for l in range(DEPTH):
        sh1, sc1, gt1, sh2, sc2, gt2 = jnp.split((jax.nn.silu(c) @ w_mod[l] + b_mod[l])[:, None, :], 6, axis=-1)
        csh1, csc1, cgt1, csh2, csc2, cgt2 = jnp.split(jax.nn.silu(c_ctx) @ w_mod[l] + b_mod[l], 6, axis=-1)

        qkv_c, z_c, ba_c, cf_c = split_mixer_inputs(modulate(rmsnorm(ctx, g_mix[l]), csh1, csc1) @ w_in[l])
        s0 = jnp.zeros((bsz, DN_HEADS, DN_DK, DN_DV), jnp.float32)
        o_c, s_fwd, s_bwd = bidir_gated_delta(
            *delta_inputs(qkv_c, ba_c, dn_conv_w[l], dn_a_log[l], dn_dt_bias[l]), s0, s0)

        qkv_x, z_x, ba_x, cf_x = split_mixer_inputs(modulate(rmsnorm(x, g_mix[l]), sh1, sc1) @ w_in[l])
        o_x, _, _ = bidir_gated_delta(
            *delta_inputs(qkv_x, ba_x, dn_conv_w[l], dn_a_log[l], dn_dt_bias[l]), s_fwd, s_bwd)
        heads_x = jnp.concatenate([
            gated_head_norm(o_x, z_x, dn_norm_g[l]),
            conformer_module(cf_x, depthwise_conv_grid_columns, cf_dw_w[l], cf_dw_b[l], cf_ln_g[l], cf_ln_b[l]),
        ], axis=-1)
        x = x + gt1 * (heads_x @ w_out[l])
        x = x + gt2 * moe_ffn(modulate(rmsnorm(x, g_ffn[l]), sh2, sc2), router_w[l], router_bias[l],
                              exp_w_gate[l], exp_w_up[l], exp_w_down[l], sh_w_gate[l], sh_w_up[l], sh_w_down[l])

        if l + 1 < DEPTH:
            heads_c = jnp.concatenate([
                gated_head_norm(o_c, z_c, dn_norm_g[l]),
                conformer_module(cf_c, depthwise_conv_seq, cf_dw_w[l], cf_dw_b[l], cf_ln_g[l], cf_ln_b[l]),
            ], axis=-1)
            ctx = ctx + cgt1 * (heads_c @ w_out[l])
            ctx = ctx + cgt2 * moe_ffn(modulate(rmsnorm(ctx, g_ffn[l]), csh2, csc2), router_w[l], router_bias[l],
                                       exp_w_gate[l], exp_w_up[l], exp_w_down[l],
                                       sh_w_gate[l], sh_w_up[l], sh_w_down[l])
    return rmsnorm(x, g_final)


SSM_GROUP = 16
SSM_WIDTH = D_MODEL // 2
SSM_GROUPS = SSM_WIDTH // SSM_GROUP
SSM_STATE = 64
CONV_WIDTH = D_MODEL
CONV_K = 3
D_FF = 4 * D_MODEL
NORM_EPS = 1e-6
DT_MIN = 1e-3
DT_MAX = 1e-1
SPLIT_SIZES = (SSM_WIDTH, CONV_WIDTH, CONV_WIDTH, CONV_WIDTH, D_MODEL, D_MODEL)
IN_COLS = sum(SPLIT_SIZES)
SPLIT_POINTS = tuple(int(v) for v in np.cumsum(SPLIT_SIZES)[:-1])


def rmsnorm_2(x, g):
    xf = x.astype(jnp.float32)
    var = jnp.mean(xf * xf, axis=-1, keepdims=True)
    return (xf * lax.rsqrt(var + NORM_EPS) * g.astype(jnp.float32)).astype(x.dtype)

def _ssm_combine(e1, e2):
    a1r, a1i, b1r, b1i = e1
    a2r, a2i, b2r, b2i = e2
    ar = a1r * a2r - a1i * a2i
    ai = a1r * a2i + a1i * a2r
    br = a2r * b1r - a2i * b1i + b2r
    bi = a2r * b1i + a2i * b1r + b2i
    return (ar, ai, br, bi)

def s5_branch(u, lam_re, lam_im, log_dt, b_re, b_im, c_re, c_im, d_skip):
    f32 = jnp.float32
    bsz, seq, _ = u.shape
    uf = u.astype(f32).reshape(bsz, seq, SSM_GROUPS, SSM_GROUP)
    lr = lam_re.astype(f32)
    li = lam_im.astype(f32)
    dt = jnp.exp(log_dt.astype(f32))[:, None]
    mag = jnp.exp(lr * dt)
    ab_re = mag * jnp.cos(li * dt)
    ab_im = mag * jnp.sin(li * dt)
    er = ab_re - 1.0
    ei = ab_im
    den = lr * lr + li * li
    q_re = (er * lr + ei * li) / den
    q_im = (ei * lr - er * li) / den
    br = b_re.astype(f32)
    bi = b_im.astype(f32)
    bb_re = q_re[..., None] * br - q_im[..., None] * bi
    bb_im = q_re[..., None] * bi + q_im[..., None] * br
    bu_re = jnp.einsum('gnc,bsgc->bsgn', bb_re, uf)
    bu_im = jnp.einsum('gnc,bsgc->bsgn', bb_im, uf)
    a_re = jnp.broadcast_to(ab_re[None, None], (1, seq, SSM_GROUPS, SSM_STATE))
    a_im = jnp.broadcast_to(ab_im[None, None], (1, seq, SSM_GROUPS, SSM_STATE))
    _, _, s_re, s_im = lax.associative_scan(_ssm_combine, (a_re, a_im, bu_re, bu_im), axis=1)
    y = (jnp.einsum('gcn,bsgn->bsgc', c_re.astype(f32), s_re)
         - jnp.einsum('gcn,bsgn->bsgc', c_im.astype(f32), s_im))
    y = y + d_skip.astype(f32).reshape(SSM_GROUPS, SSM_GROUP) * uf
    return y.reshape(bsz, seq, SSM_WIDTH)

def causal_short_conv(v, w, b):
    seq = v.shape[1]
    vp = jnp.pad(v, ((0, 0), (CONV_K - 1, 0), (0, 0)))
    out = b
    for k in range(CONV_K):
        out = out + w[k] * vp[:, k:k + seq]
    return out

def mixer_block(xn, w_in, b_in, lam_re, lam_im, log_dt, b_re, b_im, c_re, c_im, d_skip,
                w_glu_a, w_glu_b, conv_w, conv_b, w_conv_out, w_out):
    proj = jnp.einsum('bsd,de->bse', xn, w_in) + b_in
    u_ssm, c_bgate, c_cgate, c_val, g_ssm, g_conv = jnp.split(proj, SPLIT_POINTS, axis=-1)
    y_ssm = s5_branch(u_ssm, lam_re, lam_im, log_dt, b_re, b_im, c_re, c_im, d_skip).astype(xn.dtype)
    z = jax.nn.gelu(y_ssm)
    y_a = jnp.einsum('bse,ed->bsd', z, w_glu_a) * jax.nn.sigmoid(jnp.einsum('bse,ed->bsd', z, w_glu_b))
    y_b = jnp.einsum('bse,ed->bsd', c_bgate * causal_short_conv(c_cgate * c_val, conv_w, conv_b), w_conv_out)
    merged = jax.nn.sigmoid(g_ssm) * y_a + jax.nn.sigmoid(g_conv) * y_b
    return jnp.einsum('bsd,de->bse', merged, w_out)

def squared_relu_mlp(xn, w_ff1, w_ff2):
    h = jax.nn.relu(jnp.einsum('bsd,df->bsf', xn, w_ff1))
    return jnp.einsum('bsf,fd->bsd', h * h, w_ff2)

def second_inputs(seed: int = 0) -> dict:
    key = jax.random.key(seed)
    ks = jax.random.split(key, 24)
    L, D, G, N, C = DEPTH, D_MODEL, SSM_GROUPS, SSM_STATE, SSM_GROUP
    nrm = jax.random.normal
    x = nrm(ks[0], (BATCH, SEQ, D), jnp.float32)
    norm_mix_g = 1.0 + 0.02 * nrm(ks[1], (L, D), jnp.float32)
    w_in = nrm(ks[2], (L, D, IN_COLS), jnp.float32) * D ** -0.5
    b_in = 0.02 * nrm(ks[3], (L, IN_COLS), jnp.float32)
    n_idx = jnp.arange(N, dtype=jnp.float32)
    lam_re = -0.5 + 0.01 * nrm(ks[4], (L, G, N), jnp.float32)
    lam_im = math.pi * n_idx[None, None, :] + 0.01 * nrm(ks[5], (L, G, N), jnp.float32)
    log_dt = jax.random.uniform(ks[6], (L, G), jnp.float32, math.log(DT_MIN), math.log(DT_MAX))
    ssm_b_re = nrm(ks[7], (L, G, N, C), jnp.float32) * (2.0 * C) ** -0.5
    ssm_b_im = nrm(ks[8], (L, G, N, C), jnp.float32) * (2.0 * C) ** -0.5
    ssm_c_re = nrm(ks[9], (L, G, C, N), jnp.float32) * (2.0 * N) ** -0.5
    ssm_c_im = nrm(ks[10], (L, G, C, N), jnp.float32) * (2.0 * N) ** -0.5
    ssm_d = 1.0 + 0.1 * nrm(ks[11], (L, SSM_WIDTH), jnp.float32)
    w_glu_a = nrm(ks[12], (L, SSM_WIDTH, D), jnp.float32) * SSM_WIDTH ** -0.5
    w_glu_b = nrm(ks[13], (L, SSM_WIDTH, D), jnp.float32) * SSM_WIDTH ** -0.5
    conv_w = nrm(ks[14], (L, CONV_K, CONV_WIDTH), jnp.float32) * CONV_K ** -0.5
    conv_b = 0.02 * nrm(ks[15], (L, CONV_WIDTH), jnp.float32)
    w_conv_out = nrm(ks[16], (L, CONV_WIDTH, D), jnp.float32) * CONV_WIDTH ** -0.5
    w_out = nrm(ks[17], (L, D, D), jnp.float32) * D ** -0.5
    norm_mlp_g = 1.0 + 0.02 * nrm(ks[18], (L, D), jnp.float32)
    w_ff1 = nrm(ks[19], (L, D, D_FF), jnp.float32) * D ** -0.5
    w_ff2 = nrm(ks[20], (L, D_FF, D), jnp.float32) * D_FF ** -0.5
    norm_final_g = 1.0 + 0.02 * nrm(ks[21], (D,), jnp.float32)
    return {"x": x, "norm_mix_g": norm_mix_g, "w_in": w_in, "b_in": b_in,
            "lam_re": lam_re, "lam_im": lam_im, "log_dt": log_dt,
            "ssm_b_re": ssm_b_re, "ssm_b_im": ssm_b_im, "ssm_c_re": ssm_c_re, "ssm_c_im": ssm_c_im,
            "ssm_d": ssm_d, "w_glu_a": w_glu_a, "w_glu_b": w_glu_b,
            "conv_w": conv_w, "conv_b": conv_b, "w_conv_out": w_conv_out, "w_out": w_out,
            "norm_mlp_g": norm_mlp_g, "w_ff1": w_ff1, "w_ff2": w_ff2, "norm_final_g": norm_final_g}

def second_block(x, norm_mix_g, w_in, b_in, lam_re, lam_im, log_dt, ssm_b_re, ssm_b_im, ssm_c_re, ssm_c_im,
              ssm_d, w_glu_a, w_glu_b, conv_w, conv_b, w_conv_out, w_out, norm_mlp_g, w_ff1, w_ff2,
              norm_final_g):
    h = x
    for l in range(DEPTH):
        xn = rmsnorm_2(h, norm_mix_g[l])
        h = h + mixer_block(xn, w_in[l], b_in[l], lam_re[l], lam_im[l], log_dt[l],
                            ssm_b_re[l], ssm_b_im[l], ssm_c_re[l], ssm_c_im[l], ssm_d[l],
                            w_glu_a[l], w_glu_b[l], conv_w[l], conv_b[l], w_conv_out[l], w_out[l])
        xn = rmsnorm_2(h, norm_mlp_g[l])
        h = h + squared_relu_mlp(xn, w_ff1[l], w_ff2[l])
    return rmsnorm_2(h, norm_final_g)


def setup_inputs(seed=0):
    out = dict(first_inputs(seed))
    for name, value in second_inputs(seed + 1).items():
        if name != "x":
            out[name + "_2"] = value
    return out


def reference(
    x, c, ctx, c_ctx, w_mod, b_mod, g_mix, g_ffn, w_in, w_out, dn_conv_w, dn_a_log, dn_dt_bias,
    dn_norm_g, cf_dw_w, cf_dw_b, cf_ln_g, cf_ln_b, router_w, router_bias, exp_w_gate, exp_w_up,
    exp_w_down, sh_w_gate, sh_w_up, sh_w_down, g_final, norm_mix_g_2, w_in_2, b_in_2, lam_re_2,
    lam_im_2, log_dt_2, ssm_b_re_2, ssm_b_im_2, ssm_c_re_2, ssm_c_im_2, ssm_d_2, w_glu_a_2,
    w_glu_b_2, conv_w_2, conv_b_2, w_conv_out_2, w_out_2, norm_mlp_g_2, w_ff1_2, w_ff2_2,
    norm_final_g_2,
):
    x = first_block(
        x, c, ctx, c_ctx, w_mod, b_mod, g_mix, g_ffn, w_in, w_out, dn_conv_w, dn_a_log,
        dn_dt_bias, dn_norm_g, cf_dw_w, cf_dw_b, cf_ln_g, cf_ln_b, router_w, router_bias,
        exp_w_gate, exp_w_up, exp_w_down, sh_w_gate, sh_w_up, sh_w_down, g_final,
    )
    return second_block(
        x, norm_mix_g_2, w_in_2, b_in_2, lam_re_2, lam_im_2, log_dt_2, ssm_b_re_2, ssm_b_im_2,
        ssm_c_re_2, ssm_c_im_2, ssm_d_2, w_glu_a_2, w_glu_b_2, conv_w_2, conv_b_2, w_conv_out_2,
        w_out_2, norm_mlp_g_2, w_ff1_2, w_ff2_2, norm_final_g_2,
    )


_drawn_inputs = setup_inputs


def setup_inputs(seed=0):
    import zlib

    import numpy as np

    out = dict(_drawn_inputs(seed))
    spreads = {}
    factors = {'c_ctx': 3.91,
     'cf_ln_g': 2.912,
     'cf_ln_b': 3.62,
     'norm_mix_g_2': 3.038,
     'b_in_2': 3.031,
     'lam_re_2': 64.0,
     'lam_im_2': 38.272,
     'log_dt_2': 39.616,
     'ssm_b_re_2': 54.24,
     'ssm_b_im_2': 54.4,
     'ssm_c_re_2': 54.728,
     'ssm_c_im_2': 53.432,
     'conv_b_2': 24.565,
     'norm_mlp_g_2': 12.962,
     'norm_final_g_2': 8.083,
     'ssm_d_2': 8.0}
    for name, (base, spread) in spreads.items():
        noise = np.random.default_rng([zlib.crc32(name.encode()), seed]).standard_normal(out[name].shape)
        drawn = base * np.exp(spread * noise) if base else spread * noise
        out[name] = jnp.asarray(drawn.astype(out[name].dtype))
    for name, factor in factors.items():
        out[name] = (out[name] * factor).astype(out[name].dtype)
    return out
```

```python
import concourse.bass as bass
from concourse import mybir
from contextlib import ExitStack

F32 = mybir.dt.float32
U32 = mybir.dt.uint32
I32 = mybir.dt.int32
ALU = mybir.AluOpType
ACT = mybir.ActivationFunctionType
AX = mybir.AxisListType

P = 128
D = 1024
KD = D // P
T_X, T_C = 512, 256
NT_X, NT_C = T_X // P, T_C // P
NT = NT_X + NT_C
HEADS = 4
HP = HEADS * P
CHUNK = 64
CONV_K = 7
PAD = CONV_K // 2
LC = T_C + PAD + T_X
CF_K = 31
CF_ROWS, CF_W = 8, 64
EPS = 1e-6
LEVELS = [2, 4, 8, 16, 32]
N_EXP, TOP_K, N_GRP, GRP, KEEP_GRP = 64, 6, 8, 8, 4
F_EXP = 256
ROUTED_SCALE = 2.5
PI2_B = 2029 / 2 ** 20
PI2_C = 3.0199159795074593e-07
EXPW = KD * 2 * F_EXP + 2 * D

COLS = {}
_at = 0
for _name, _n in [("g_mix", KD), ("b_mod", 16), ("dn_norm_g", 1), ("conv_w", 12 * CONV_K), ("cf_w", 4 * CF_K),
                  ("cf_b", 4), ("cf_g", 4), ("cf_lb", 4), ("w_ba", KD * 16)]:
    COLS[_name] = (_at, _n)
    _at += _n
N_COLS = _at
COLS2 = {}
_at = 0
for _name, _n in [("router_w", KD * N_EXP),
                  ("g2", KD), ("b_in2", 44), ("conv_w2", KD * 3), ("conv_b2", KD), ("gmlp", KD), ("ssm_d", 4),
                  ("lam_re", 16), ("lam_im", 16), ("log_dt", 16)]:
    COLS2[_name] = (_at, _n)
    _at += _n
N_COLS2 = _at
ROWS = {}
_at = 0
for _name, _n in [("a_log", 8), ("dt_bias", 8), ("router_bias", N_EXP), ("g_ffn", D), ("g_final", D), ("g_final2", D)]:
    ROWS[_name] = (_at, _n)
    _at += _n
N_ROWS = _at


PHASES = ("mixer", "experts", "second")


def build(nc, a, out, h2d, yd):
    ctx = ExitStack()
    with ctx:
        arena = ctx.enter_context(nc.sbuf_tensor("arena", [P, 53184], F32))
        sems = {}
        phase = [0]

        def S(name):
            if name not in sems:
                sems[name] = nc.alloc_semaphore(f"{PHASES[phase[0]]}_{name}")
            return sems[name]

        top = [0]

        def at(off, n):
            assert off + n <= 53184, (off, n)
            top[0] = max(top[0], off + n)
            return arena[:, off:off + n]

        bank = [ctx.enter_context(nc.psum_tensor(f"bank{i}", [P, 512], F32)) for i in range(8)]

        WCH = KD * 512
        RING = 3
        ring = [at(WCH * i, WCH) for i in range(RING)]
        o = RING * WCH
        hT = at(o, KD * (T_C + T_X)).rearrange("p (k t) -> p k t", k=KD)
        tmpA = o
        o += KD * (T_C + T_X)
        qkvT = at(o, 12 * LC).rearrange("p (m t) -> p m t", m=12)
        o_acc = at(o + 8 * LC, NT_X * HP).rearrange("p (t c) -> p t c", t=NT_X)
        state = at(o + 8 * LC + NT_X * HP, 2 * HP).rearrange("p (d c) -> p d c", d=2)
        o += 12 * LC
        x_raw = at(o, NT * D).rearrange("p (t d) -> p t d", t=NT)
        kn = at(o, NT * HP).rearrange("p (t c) -> p t c", t=NT)
        vt = at(o + NT * HP, NT * HP).rearrange("p (t c) -> p t c", t=NT)
        qn = at(o + 2 * NT * HP, NT_X * HP).rearrange("p (t c) -> p t c", t=NT_X)
        o += 2 * NT * HP + NT_X * HP
        modrow = at(o, 4 * D).rearrange("p (r d) -> p r d", r=4)
        o += 4 * D
        sz = at(o, 4 * 512).rearrange("p (h t) -> p h t", h=4)
        o += 4 * 512
        yc = at(o, 4 * 512).rearrange("p (h t) -> p h t", h=4)
        o += 4 * 512
        cols = at(o, N_COLS)
        o += N_COLS
        ident = at(o, P); o += P
        ones = at(o, P); o += P
        upto = at(o, 2 * P).rearrange("p (d c) -> p d c", d=2); o += 2 * P
        lvl = at(o, 2 * 6 * P).rearrange("p (d l c) -> p d l c", d=2, l=6); o += 12 * P
        small = at(o, 640); o += 640
        TB = o
        lane_at = [2 * WCH, 2 * WCH + 8 * 512] + [tmpA]
        free = [(2 * WCH, WCH), (tmpA, KD * (T_C + T_X)), (TB, 53184 - TB)]
        blocks = []
        for off, n in free:
            blocks += [off + 512 * i for i in range(n // 512)]
        assert len(blocks) >= 30, (len(blocks), TB, 53184 - TB)
        names = ["et", "lt", "x", "y", "t1", "ct", "kb", "kbg", "vb", "u", "wT", "qdT", "it", "kd", "vn"]
        lane = [{nm: at(blocks[15 * l + i], 512) for i, nm in enumerate(names)} for l in range(2)]

        def h4(ap):
            return ap.rearrange("p (h c) -> p h c", h=HEADS)

        def col(name, i=0, n=1):
            s, _ = COLS[name]
            return cols[:, s + i:s + i + n]

        sm = [0]

        def take(n):
            sm[0] += n
            assert sm[0] <= 640
            return small[:, sm[0] - n:sm[0]]

        cs = take(16).rearrange("p (k s) -> p k s", k=KD)
        ss, rt, rs = take(NT), take(NT), take(NT)
        mc = take(32).rearrange("p (i s) -> p i s", s=2)
        scg = take(16).rearrange("p (k s) -> p k s", s=2)
        ba = take(NT * 16).rearrange("p (t d w h) -> p t d w h", t=NT, d=2, w=2)
        beta = take(NT * 8).rearrange("p (t d h) -> p t d h", t=NT, d=2)
        gg = take(NT * 8).rearrange("p (t d h) -> p t d h", t=NT, d=2)
        g1 = take(NT * 8).rearrange("p (t d h) -> p t d h", t=NT, d=2)
        g2 = take(NT * 8).rearrange("p (t d h) -> p t d h", t=NT, d=2)
        nal = take(8)
        ssq = take(8)
        rq = take(8)
        rq2 = take(8)
        gcs = [take(4), take(4)]
        eg = [take(4), take(4)]
        gl = [take(8).rearrange("p (h c) -> p h c", c=2) for _ in range(2)]
        kdl = [take(4).rearrange("p (h o) -> p h o", o=1) for _ in range(2)]
        so = take(16); so2 = take(16); so3 = take(16)
        rowb = take(16)
        eps1, epsP, one1 = take(1), take(1), take(1)
        sq_cf = at(WCH + 2048, 2048).rearrange("p (j t) -> p j t", j=4)
        cv = ring[1][:, 0:2048].rearrange("p (j t) -> p j t", j=4)
        o = RING * WCH + KD * (T_C + T_X) + 12 * LC
        xr = at(o, NT_X * D).rearrange("p (t d) -> p t d", t=NT_X)
        heads = at(o + 4096, KD * T_X).rearrange("p (k t) -> p k t", k=KD)
        h2 = at(o + 4096, NT_X * D).rearrange("p (t d) -> p t d", t=NT_X)
        h2T = at(o + 12288, KD * T_X).rearrange("p (k t) -> p k t", k=KD)
        sq4 = at(tmpA, 2048)
        cen = at(tmpA + 2048, 2048).rearrange("p (j t) -> p j t", j=4)
        onr = at(tmpA + 4096, 2048)
        rst = at(2 * WCH, 512)
        gtmp = [at(2 * WCH + 512 + 512 * i, 512) for i in range(2)]
        gffn = at(2 * WCH + 2048, D)
        cols2 = at(TB, N_COLS2)
        o = TB + N_COLS2

        def col2(name, i=0, n=1):
            b, _ = COLS2[name]
            return cols2[:, b + i:b + i + n]
        padb = [at(TB + 784 * i, LC + 2 * PAD) for i in range(2)]
        acc = [at(TB + 1568 + 784 * i, LC) for i in range(2)]
        csb = at(TB, KD * P).rearrange("p (k c) -> p k c", k=KD)
        sg_t = at(TB + 3136, 512)
        junk = [at(tmpA + D * i, D) for i in range(2)]
        tokT = slice(T_C, T_C + T_X)

        def bc(ap, shape):
            return ap.to_broadcast(shape)

        n_w = 20
        PAIRS = [((0, p), (1, [1, 0, 5, 4, 3, 2][p])) for p in range(6)]

        def tok(t):
            s = t * P if t < NT_C else PAD + t * P
            return slice(s, s + P)


        def end_phase():
            nc.all_engine_barrier()
            nc.clear_and_free_semaphores(list(sems.values()))
            nc.all_engine_barrier()
            sems.clear()
            phase[0] += 1

        with nc.Block() as block:

            @block.sync
            def _(sp):
                sp.dma_start(cs, a["cT"]).then_inc(S("c_in"), 16)
                sp.dma_start(cols, a["cols"]).then_inc(S("cols_in"), 16)

                def spent(n):
                    if n < 4:
                        return S("modcol_mm"), n + 1
                    if n < 12:
                        return S("modrow_mm"), n - 3
                    if n < 15:
                        return S("qkv_mm"), 4 * (n - 11)
                    return S("zcf_mm"), 4 * (n - 14)

                def wload(n):
                    if n >= RING:
                        sp.wait_ge(*spent(n - RING))
                    src = a["wmod"][n] if n < 12 else a["win"][n - 12] if n < 18 else a["wout"][n - 18]
                    sp.dma_start(ring[n % RING], src).then_inc(S(f"w_in{n % RING}"), 16)
                wload(0)
                sp.dma_start(x_raw[:, 0:NT_C, :], a["ctx"].rearrange("(t p) d -> p t d", p=P)).then_inc(S("x_in"), 16)
                sp.dma_start(x_raw[:, NT_C:NT, :], a["x"].rearrange("(t p) d -> p t d", p=P)).then_inc(S("x_in"), 16)
                sp.dma_start(modrow.rearrange("p r d -> p (r d)"), a["b_mod_row"].partition_broadcast(P)).then_inc(S("mb_in"), 16)
                sp.dma_start(rowb, a["rows"][0:16].partition_broadcast(P)).then_inc(S("row_in"), 16)
                for n in range(1, n_w - 1):
                    wload(n)
                for l in range(2):
                    sp.wait_ge(S(f"scan_ev{l}"), 12)
                    sp.wait_ge(S(f"kd{l}"), 6)
                sp.dma_start(xr, a["x"].rearrange("(t p) d -> p t d", p=P)).then_inc(S("xr_in"), 16)
                sp.wait_ge(S("cf_sqsum"), 1)
                wload(n_w - 1)
            @block.tensor
            def _(pe):
                def arrived(n):
                    pe.wait_ge(S(f"w_in{n % RING}"), 16 * (n // RING + 1))
                    return ring[n % RING].rearrange("p (k c) -> p k c", k=KD)

                pe.wait_ge(S("cs"), 1)
                for n in range(4):
                    w = arrived(n)
                    for m in range(4):
                        i = n * 4 + m
                        for k in range(KD):
                            mm = pe.matmul(bank[0][:, 2 * i:2 * i + 2], w[:, k, m * P:(m + 1) * P], cs[:, k, :],
                                           start=(k == 0), stop=(k == KD - 1))
                    mm.then_inc(S("modcol_mm"), 1)
                pe.wait_ge(S("ident"), 2)
                for u in range(2 * KD):
                    k = u // 2
                    tiles = range(NT_C, NT) if u % 2 == 0 else range(NT_C)
                    if u < 1:
                        pe.wait_ge(S("xn"), NT)
                    if u >= 4:
                        pe.wait_ge(S("hT"), u - 3)
                    for j, t in enumerate(tiles):
                        mm = pe.transpose(bank[1 + u % 4][:, j * P:(j + 1) * P], x_raw[:, t, k * P:(k + 1) * P], ident)
                    mm.then_inc(S("tp_mm"), 1)
                pe.wait_ge(S("csb"), 1)
                for r in range(8):
                    w = arrived(4 + r)
                    if r >= 3:
                        pe.wait_ge(S("modrow"), r - 2)
                    for k in range(KD):
                        mm = pe.matmul(bank[5 + r % 3][:, :], csb[:, k, :], w[:, k, :], start=(k == 0), stop=(k == KD - 1))
                    mm.then_inc(S("modrow_mm"), 1)
                pe.wait_ge(S("hT"), 2 * KD)
                wba = col("w_ba", 0, KD * 16).rearrange("p (k c) -> p k c", k=KD)
                pe.wait_ge(S("modcol"), 1)
                for t in range(NT):
                    for k in range(KD):
                        mm = pe.matmul(bank[0][:, t * 16:(t + 1) * 16], hT[:, k, t * P:(t + 1) * P], wba[:, k, :],
                                       start=(k == 0), stop=(k == KD - 1))
                mm.then_inc(S("ba_mm"), 1)
                for m in range(12):
                    if m % 4 == 0:
                        w = arrived(12 + m // 4)
                    bx, bcx = bank[1 + 2 * (m % 2)], bank[2 + 2 * (m % 2)]
                    if m >= 2:
                        pe.wait_ge(S("qkv_cp"), 2 * (m - 1))
                    for k in range(KD):
                        lhs = w[:, k, (m % 4) * P:(m % 4 + 1) * P]
                        pe.matmul(bx[:, 0:T_X], lhs, hT[:, k, T_C:], start=(k == 0), stop=(k == KD - 1))
                        mm = pe.matmul(bcx[:, 0:T_C], lhs, hT[:, k, 0:T_C], start=(k == 0), stop=(k == KD - 1))
                    mm.then_inc(S("qkv_mm"), 1)
                pe.wait_ge(S("modrow"), 8)
                for m in range(12):
                    if m % 4 == 0:
                        w = arrived(15 + m // 4)
                    if m < 4:
                        b = bank[5 + m % 3]
                        if m == 3:
                            pe.wait_ge(S("z"), 1)
                    else:
                        j = m - 4
                        b = bank[1 + j % 4]
                        if j == 0:
                            pe.wait_ge(S("qkv_cp"), 24)
                        if j >= 4 and j % 2 == 0:
                            pe.wait_ge(S("yc"), j // 2 - 1)
                    for k in range(KD):
                        mm = pe.matmul(b[:, :], w[:, k, (m % 4) * P:(m % 4 + 1) * P], hT[:, k, T_C:],
                                       start=(k == 0), stop=(k == KD - 1))
                    mm.then_inc(S("zcf_mm"), 1)
                for t in range(NT):
                    for w3 in range(3):
                        if w3 == 0 and t < NT_C:
                            continue
                        pe.wait_ge(S("qkv_silu"), 4 * (w3 + 1))
                        if t == (NT_C if w3 == 0 else 0):
                            pe.wait_ge(S("yc"), 4)
                            pe.wait_ge(S("z"), 4)
                        if t >= 1:
                            pe.wait_ge(S("kqn"), t)
                            pe.wait_ge(S("vt"), t)
                        for h in range(HEADS):
                            mm = pe.transpose(bank[w3][:, h * P:(h + 1) * P], qkvT[:, 4 * w3 + h, tok(t)], ident)
                    mm.then_inc(S("tm_mm"), 1)
                    if t >= 1:
                        pe.wait_ge(S("kqT"), t)
                    pe.wait_ge(S("kqn"), t + 1)
                    for h in range(HEADS):
                        mm = pe.transpose(bank[3][:, h * P:(h + 1) * P], kn[:, t, h * P:(h + 1) * P], ident)
                    if t >= NT_C:
                        for h in range(HEADS):
                            mm = pe.transpose(bank[4][:, h * P:(h + 1) * P], qn[:, t - NT_C, h * P:(h + 1) * P], ident)
                    mm.then_inc(S("kqT_mm"), 1)
                pe.wait_ge(S("kqT"), NT)
                pe.wait_ge(S("vt"), NT)
                for p in range(6):
                    both = [(l, d, t) for l, (d, t) in enumerate(PAIRS[p])]
                    for l, d, t in both:
                        B = bank[4 * l:4 * l + 4]
                        pe.wait_ge(S(f"ug{l}"), p + 1)
                        if p >= 1:
                            pe.wait_ge(S(f"scan_ev{l}"), 2 * p)
                            pe.wait_ge(S(f"o_ev{l}"), 2 * (p - 2)) if p > 2 else None
                        pe.matmul(B[0][:, :], ones, lane[l]["ct"], start=True, stop=True)
                        pe.matmul(B[1][:, 0:4], upto[:, d, :], gg[:, t, d, :], start=True, stop=True).then_inc(S(f"grow{l}"), 1)
                    for l, d, t in both:
                        B, L = bank[4 * l:4 * l + 4], lane[l]
                        pe.wait_ge(S(f"kb{l}"), p + 1)
                        for h in range(HEADS):
                            mm = pe.transpose(B[2][:, h * P:(h + 1) * P], L["kb"][:, h * P:(h + 1) * P], ident)
                        mm.then_inc(S(f"kbT_mm{l}"), 1)
                        if p >= 2:
                            pe.wait_ge(S(f"qd{l}"), p - 1)
                            for h in range(HEADS):
                                mm = pe.transpose(B[3][:, h * P:(h + 1) * P], L["u"][:, h * P:(h + 1) * P], ident)
                            mm.then_inc(S(f"qdT_mm{l}"), 1)
                    for l, d, t in both:
                        B, L = bank[4 * l:4 * l + 4], lane[l]
                        pe.wait_ge(S(f"kbT{l}"), p + 1)
                        pe.wait_ge(S(f"et{l}"), p + 1)
                        for h in range(HEADS):
                            mm = pe.matmul(B[0][:, h * P:(h + 1) * P], qkvT[:, 4 + h, tok(t)], L["t1"][:, h * P:(h + 1) * P],
                                           start=True, stop=True)
                        mm.then_inc(S(f"lt_mm{l}"), 1)
                        if p >= 2:
                            for h in range(HEADS):
                                mm = pe.matmul(B[1][:, h * P:(h + 1) * P], qkvT[:, 4 + h, tok(t)], qkvT[:, h, tok(t)],
                                               start=True, stop=True)
                            mm.then_inc(S(f"it_mm{l}"), 1)
                    for l, d, t in both:
                        B, L = bank[4 * l:4 * l + 4], lane[l]
                        pe.wait_ge(S(f"y{l}"), 6 * p + 1)
                        for h in range(HEADS):
                            mm = pe.transpose(B[2][:, h * P:(h + 1) * P], L["y"][:, h * P:(h + 1) * P], ident)
                        mm.then_inc(S(f"x2_mm{l}"), 1)
                    for n, s in enumerate(LEVELS):
                        for l, d, t in both:
                            B, L = bank[4 * l:4 * l + 4], lane[l]
                            pe.wait_ge(S(f"ct{l}"), 5 * p + n + 1)
                            pe.wait_ge(S(f"x{l}"), 5 * p + n + 1)
                            for h in range(HEADS):
                                hs = slice(h * P, (h + 1) * P)
                                mm = pe.matmul(B[0][:, hs], L["ct"][:, hs], L["x"][:, hs], start=True, stop=True)
                            mm.then_inc(S(f"t1_mm{l}"), 1)
                        for l, d, t in both:
                            B, L = bank[4 * l:4 * l + 4], lane[l]
                            pe.wait_ge(S(f"t1{l}"), 5 * p + n + 1)
                            if n == 0 and p >= 2:
                                pe.wait_ge(S(f"it{l}"), p - 1)
                            pe.wait_ge(S(f"y{l}"), 6 * p + n + 1)
                            if n < 4:
                                for h in range(HEADS):
                                    hs = slice(h * P, (h + 1) * P)
                                    mm = pe.matmul(B[1][:, hs], L["y"][:, hs], L["t1"][:, hs], start=True, stop=True)
                            for h in range(HEADS):
                                hs = slice(h * P, (h + 1) * P)
                                mm = pe.matmul(B[2][:, hs], L["t1"][:, hs], L["y"][:, hs], start=True, stop=True)
                            mm.then_inc(S(f"xy_mm{l}"), 1)
                    for l, d, t in both:
                        B, L = bank[4 * l:4 * l + 4], lane[l]
                        pe.wait_ge(S(f"y{l}"), 6 * p + 6)
                        pe.wait_ge(S(f"kbg{l}"), p + 1)
                        if p >= 2:
                            pe.wait_ge(S(f"qdT{l}"), p - 1)
                        for h in range(HEADS):
                            hs = slice(h * P, (h + 1) * P)
                            pe.matmul(B[3][:, hs], L["y"][:, hs], L["vb"][:, hs], start=True, stop=True)
                        for h in range(HEADS):
                            hs = slice(h * P, (h + 1) * P)
                            mm = pe.matmul(B[0][:, hs], L["kbg"][:, hs], L["y"][:, hs], start=True, stop=True)
                        mm.then_inc(S(f"uw_mm{l}"), 1)
                    for j in range(2):
                        for l, d, t in both:
                            B, L = bank[4 * l:4 * l + 4], lane[l]
                            c = j if d == 0 else 1 - j
                            r = slice(CHUNK * c, CHUNK * c + CHUNK)
                            n = 2 * p + j
                            pe.wait_ge(S(f"uw{l}"), p + 1)
                            if n >= 1:
                                pe.wait_ge(S(f"scan_ev{l}"), n)
                            else:
                                pe.wait_ge(S("state0"), 1)
                            for h in range(HEADS):
                                hs = slice(h * P, (h + 1) * P)
                                mm = pe.matmul(B[1][r, hs], L["wT"][:, h * P + CHUNK * c:h * P + CHUNK * c + CHUNK],
                                               state[:, d, hs], start=True, stop=True)
                            mm.then_inc(S(f"ws_mm{l}"), 1)
                        for l, d, t in both:
                            B, L = bank[4 * l:4 * l + 4], lane[l]
                            c = j if d == 0 else 1 - j
                            r = slice(CHUNK * c, CHUNK * c + CHUNK)
                            n = 2 * p + j
                            pe.wait_ge(S(f"vn{l}"), n + 1)
                            pe.wait_ge(S(f"kd{l}"), p + 1)
                            for h in range(HEADS):
                                hs = slice(h * P, (h + 1) * P)
                                mm = pe.matmul(B[2][:, hs], L["kd"][r, hs], L["vn"][r, hs], start=True, stop=True)
                            if p < 2:
                                mm.then_inc(S(f"su_mm{l}"), 1)
                                continue
                            if n >= 5:
                                pe.wait_ge(S(f"o_ev{l}"), n - 4)
                            for h in range(HEADS):
                                hs = slice(h * P, (h + 1) * P)
                                cc = slice(h * P + CHUNK * c, h * P + CHUNK * c + CHUNK)
                                pe.matmul(B[3][r, hs], L["qdT"][:, cc], state[:, d, hs], start=True, stop=False,
                                          skip_group_check=True)
                                mm = pe.matmul(B[3][r, hs], L["it"][r, cc], L["vn"][r, hs], start=False, stop=True,
                                               skip_group_check=True)
                            mm.then_inc(S(f"su_mm{l}"), 1)
                pe.wait_ge(S("cv"), 4)
                for l in range(2):
                    pe.wait_ge(S(f"scan_ev{l}"), 12)
                    pe.wait_ge(S(f"o_ev{l}"), 8)
                for j in range(4):
                    mm = pe.matmul(bank[0][:, :], ones, cv[:, j, :], start=(j == 0), stop=(j == 3))
                mm.then_inc(S("cf_sum"), 1)
                pe.wait_ge(S("cf_sq"), 4)
                for j in range(4):
                    mm = pe.matmul(bank[1][:, :], ones, sq_cf[:, j, :], start=(j == 0), stop=(j == 3))
                mm.then_inc(S("cf_sqsum"), 1)
                pe.wait_ge(S("onr"), 1)
                o4 = onr.rearrange("p (t h c) -> p t h c", t=NT_X, h=HEADS)
                for h in range(HEADS):
                    for t in range(NT_X):
                        mm = pe.transpose(bank[2 + h][:, t * P:(t + 1) * P], o4[:, t, h, :], ident)
                    mm.then_inc(S("hd_mm"), 1)
                pe.wait_ge(S("hd"), 4)
                pe.wait_ge(S("cfh"), 4)
                for half in range(2):
                    w = arrived(18 + half)
                    for t in range(NT_X):
                        for k in range(KD):
                            mm = pe.matmul(bank[4 * half + t][:, :], heads[:, k, t * P:(t + 1) * P], w[:, k, :],
                                           start=(k == 0), stop=(k == KD - 1))
                        mm.then_inc(S("wo_mm"), 1)

            @block.scalar
            def _(act):
                act.wait_ge(S("c_in"), 16)
                act.activation(cs, cs, ACT.Silu).then_inc(S("cs"), 1)
                act.wait_ge(S("x_in"), 32)
                for t in range(NT):
                    if t >= 2:
                        act.wait_ge(S("ss"), t - 1)
                    act.activation(junk[t % 2], x_raw[:, t, :], ACT.Square, accum_out=ss[:, t:t + 1]).then_inc(S("ss"), 1)
                act.wait_ge(S("ss"), NT)
                act.wait_ge(S("consts"), 1)
                act.activation(rt, ss, ACT.Sqrt, scale=1.0 / D, bias=eps1).then_inc(S("rt"), 1)
                act.wait_ge(S("scg"), 1)
                for u in range(2 * KD):
                    k, s = u // 2, u % 2
                    act.wait_ge(S("tp_mm"), u + 1)
                    dst = hT[:, k, T_C:] if s == 0 else hT[:, k, 0:T_C]
                    act.activation(dst, bank[1 + u % 4][:, 0:dst.shape[1]], ACT.Identity, scale=scg[:, k, s:s + 1],
                                   bias=mc[:, k, s:s + 1]).then_inc(S("hT"), 1)
                act.wait_ge(S("padz"), 2)
                for m in range(13):
                    if m < 12:
                        act.wait_ge(S("qkv_mm"), m + 1)
                        if m >= 2:
                            act.wait_ge(S("conv"), m - 1)
                        pd = padb[m % 2]
                        act.activation(pd[:, 2 * PAD + T_C:2 * PAD + T_C + T_X], bank[1 + 2 * (m % 2)][:, 0:T_X], ACT.Copy).then_inc(S("qkv_cp"), 1)
                        act.activation(pd[:, PAD:PAD + T_C], bank[2 + 2 * (m % 2)][:, 0:T_C], ACT.Copy).then_inc(S("qkv_cp"), 1)
                    if m >= 1:
                        act.wait_ge(S("conv"), m)
                        act.activation(qkvT[:, m - 1, :], acc[(m - 1) % 2], ACT.Silu).then_inc(S("qkv_silu"), 1)
                for m in range(4):
                    act.wait_ge(S("zcf_mm"), m + 1)
                    act.activation(sz[:, m, :], bank[5 + m % 3][:, :], ACT.Silu).then_inc(S("z"), 1)
                for j in range(4):
                    act.wait_ge(S("zcf_mm"), 4 + 2 * j + 2)
                    if j >= 1:
                        act.wait_ge(S("yc"), j)
                    act.activation(sg_t, bank[1 + (2 * j + 1) % 4][:, :], ACT.Sigmoid).then_inc(S("cfs"), 1)
                act.wait_ge(S("ba"), 1)
                act.activation(beta, ba[:, :, :, 0, :], ACT.Sigmoid).then_inc(S("beta"), 1)
                act.wait_ge(S("g_a"), 1)
                act.activation(g2, g2, ACT.Exp).then_inc(S("g_b"), 1)
                act.wait_ge(S("g_b"), 1)
                act.activation(g2, g2, ACT.Ln, bias=one1).then_inc(S("g_b"), 1)
                act.wait_ge(S("row_in"), 16)
                act.activation(nal, rowb[:, 0:8], ACT.Exp).then_inc(S("g_b"), 1)
                for t in range(NT):
                    act.wait_ge(S("tm_mm"), t + 1)
                    if t >= 1:
                        act.wait_ge(S("kqn"), t)
                    act.activation(h4(lane[0]["et"]), h4(bank[1][:, :]), ACT.Square).then_inc(S("sq"), 1)
                    if t >= NT_C:
                        act.activation(h4(lane[1]["et"]), h4(bank[0][:, :]), ACT.Square).then_inc(S("sq"), 1)
                    act.activation(vt[:, t, :], bank[2][:, :], ACT.Copy).then_inc(S("vt"), 1)
                    act.wait_ge(S("ssq"), t + 1)
                    act.activation(rq[:, 0:4], ssq[:, 0:4], ACT.Sqrt, bias=eps1).then_inc(S("rq"), 1)
                    act.activation(rq[:, 4:8], ssq[:, 4:8], ACT.Sqrt, scale=float(P), bias=epsP).then_inc(S("rq"), 1)
                    act.wait_ge(S("kqT_mm"), t + 1)
                    ins = act.activation(qkvT[:, 4:8, tok(t)], h4(bank[3][:, :]), ACT.Copy)
                    if t >= NT_C:
                        ins = act.activation(qkvT[:, 0:4, tok(t)], h4(bank[4][:, :]), ACT.Copy)
                    ins.then_inc(S("kqT"), 1)
                for p in range(6):
                    both = [(l, d, t) for l, (d, t) in enumerate(PAIRS[p])]
                    for l, d, t in both:
                        B, L = bank[4 * l:4 * l + 4], lane[l]
                        act.wait_ge(S(f"gc{l}"), p + 1)
                        act.activation(eg[l], gcs[l], ACT.Exp).then_inc(S(f"eg{l}"), 1)
                        act.activation(gl[l], gl[l], ACT.Exp).then_inc(S(f"gl{l}"), 1)
                        act.wait_ge(S(f"dd{l}"), p + 1)
                        act.activation(L["lt"], L["et"], ACT.Exp).then_inc(S(f"ex{l}"), 1)
                    for l, d, t in both:
                        B, L = bank[4 * l:4 * l + 4], lane[l]
                        act.wait_ge(S(f"kbT_mm{l}"), p + 1)
                        act.activation(L["t1"], B[2][:, :], ACT.Copy).then_inc(S(f"kbT{l}"), 1)
                        if p >= 2:
                            act.wait_ge(S(f"qdT_mm{l}"), p - 1)
                            act.activation(L["qdT"], B[3][:, :], ACT.Copy).then_inc(S(f"qdT{l}"), 1)
                    for l, d, t in both:
                        B, L = bank[4 * l:4 * l + 4], lane[l]
                        act.wait_ge(S(f"x2_mm{l}"), p + 1)
                        act.activation(L["x"], B[2][:, :], ACT.Copy).then_inc(S(f"x{l}"), 1)
                    for n in range(5):
                        for l, d, t in both:
                            B, L = bank[4 * l:4 * l + 4], lane[l]
                            act.wait_ge(S(f"t1_mm{l}"), 5 * p + n + 1)
                            act.activation(L["t1"], B[0][:, :], ACT.Copy).then_inc(S(f"t1{l}"), 1)
                    for l, d, t in both:
                        B, L = bank[4 * l:4 * l + 4], lane[l]
                        act.wait_ge(S(f"uw_mm{l}"), p + 1)
                        act.activation(L["wT"], B[0][:, :], ACT.Copy)
                        act.activation(L["u"], B[3][:, :], ACT.Copy).then_inc(S(f"uw{l}"), 1)
                    if p >= 2:
                        for j in range(2):
                            for l, d, t in both:
                                B, L = bank[4 * l:4 * l + 4], lane[l]
                                c = j if d == 0 else 1 - j
                                r = slice(CHUNK * c, CHUNK * c + CHUNK)
                                first = (p - 2 < 2)
                                if not first:
                                    continue
                                act.wait_ge(S(f"su_mm{l}"), 2 * p + j + 1)
                                act.activation(o_acc[r, t - NT_C, :], B[3][r, :], ACT.Copy).then_inc(S(f"o_ev{l}"), 1)

                for l in range(2):
                    act.wait_ge(S(f"o_ev{l}"), 8)
                act.activation(sq4, o_acc.rearrange("p t c -> p (t c)"), ACT.Square).then_inc(S("osq"), 1)
                act.wait_ge(S("ossq"), 1)
                act.activation(so, so, ACT.Sqrt, scale=1.0 / P, bias=eps1).then_inc(S("orq"), 1)
                act.wait_ge(S("onr"), 1)
                for j in range(4):
                    act.wait_ge(S("cen"), j + 1)
                    act.activation(sq_cf[:, j, :], cen[:, j, :], ACT.Square).then_inc(S("cf_sq"), 1)
                act.wait_ge(S("cf_sqsum"), 1)
                act.activation(rst, bank[1][:, :], ACT.Sqrt, scale=1.0 / 512, bias=eps1).then_inc(S("cf_rt"), 1)
                for j in range(4):
                    act.wait_ge(S("cfn"), j + 1)
                    act.activation(heads[:, 4 + j, :], cen[:, j, :], ACT.Silu, scale=col("cf_g", j), bias=col("cf_lb", j)).then_inc(S("cfh"), 1)


            @block.vector
            def _(dve):
                count = {}

                def link(ins, signal="dve_chain"):
                    count[signal] = count.get(signal, 0) + 1
                    ins.then_inc(S(signal), 1)
                    dve.wait_ge(S(signal), count[signal])

                dve.memset(eps1, EPS)
                dve.memset(epsP, EPS * P)
                dve.memset(one1, 1.0).then_inc(S("consts"), 1)
                dve.wait_ge(S("cs"), 1)
                dve.tensor_copy(csb, bc(cs[:, :, 0:1], [P, KD, P])).then_inc(S("csb"), 1)
                dve.wait_ge(S("rt"), 1)
                link(dve.reciprocal(rs, rt))
                for t in range(NT):
                    dve.tensor_scalar(x_raw[:, t, :], x_raw[:, t, :], rs[:, t:t + 1], None, ALU.mult).then_inc(S("xn"), 1)
                dve.wait_ge(S("modcol_mm"), 4)
                dve.wait_ge(S("cols_in"), 16)
                pm = bank[0][:, 0:32].rearrange("p (i s) -> p i s", s=2)
                bm = col("b_mod", 0, 16).rearrange("p (i o) -> p i o", o=1)
                link(dve.tensor_tensor(mc, pm, bc(bm, [P, 16, 2]), ALU.add), "modcol")
                link(dve.tensor_scalar(scg, mc[:, 8:16, :], 1.0, None, ALU.add))
                gm = col("g_mix", 0, 8).rearrange("p (i o) -> p i o", o=1)
                dve.tensor_tensor(scg, scg, bc(gm, [P, 8, 2]), ALU.mult).then_inc(S("scg"), 1)
                dve.wait_ge(S("mb_in"), 16)
                mr = modrow.rearrange("p r d -> p (r d)")
                for r in range(8):
                    dve.wait_ge(S("modrow_mm"), r + 1)
                    dve.tensor_tensor(mr[:, r * 512:(r + 1) * 512], bank[5 + r % 3][:, :], mr[:, r * 512:(r + 1) * 512],
                                      ALU.add).then_inc(S("modrow"), 1)
                dve.wait_ge(S("ba_mm"), 1)
                link(dve.tensor_copy(ba.rearrange("p t d w h -> p (t d w h)"), bank[0][:, 0:NT * 16]), "ba")
                dve.wait_ge(S("row_in"), 16)
                db = rowb[:, 8:16].rearrange("p (o d h) -> p o d h", o=1, d=2)
                for t in range(NT):
                    ins = dve.tensor_tensor(g1[:, t, :, :], ba[:, t, :, 1, :], db[:, 0, :, :], ALU.add)
                link(ins)
                for i in range(2):
                    dve.memset(padb[i][:, 0:PAD], 0.0)
                    dve.memset(padb[i][:, PAD + T_C:2 * PAD + T_C], 0.0)
                    dve.memset(padb[i][:, 2 * PAD + T_C + T_X:], 0.0).then_inc(S("padz"), 1)
                link(dve.tensor_scalar(g2, g1, 0.0, 2.0, ALU.max, ALU.mult))
                link(dve.tensor_tensor(g2, g1, g2, ALU.subtract))
                link(dve.tensor_scalar(g1, g1, 0.0, None, ALU.max), "g_a")
                def column_conv(j):
                    if j == 0:
                        dve.wait_ge(S("zcf_mm"), 8)
                    dve.wait_ge(S("yc"), j + 1)
                    mid = CF_K // 2
                    link(dve.tensor_scalar(cv[:, j, :], yc[:, j, :], col("cf_w", j * CF_K + mid), col("cf_b", j), ALU.mult, ALU.add))
                    for off in range(1, CF_ROWS):
                        n = (CF_ROWS - off) * CF_W
                        link(dve.scalar_tensor_tensor(out=cv[:, j, 0:n], in0=yc[:, j, off * CF_W:], scalar=col("cf_w", j * CF_K + mid + off),
                                                      in1=cv[:, j, 0:n], op0=ALU.mult, op1=ALU.add))
                        ins = dve.scalar_tensor_tensor(out=cv[:, j, off * CF_W:], in0=yc[:, j, 0:n], scalar=col("cf_w", j * CF_K + mid - off),
                                                       in1=cv[:, j, off * CF_W:], op0=ALU.mult, op1=ALU.add)
                        if off < CF_ROWS - 1:
                            link(ins)
                    ins.then_inc(S("cv"), 1)

                for m in range(12):
                    dve.wait_ge(S("qkv_cp"), 2 * (m + 1))
                    if m >= 2:
                        dve.wait_ge(S("qkv_silu"), m - 1)
                    pd, ac = padb[m % 2], acc[m % 2]
                    link(dve.tensor_scalar(ac, pd[:, 0:LC], col("conv_w", m * CONV_K), None, ALU.mult))
                    for i in range(1, CONV_K):
                        ins = dve.scalar_tensor_tensor(out=ac, in0=pd[:, i:i + LC], scalar=col("conv_w", m * CONV_K + i),
                                                       in1=ac, op0=ALU.mult, op1=ALU.add)
                        if i < CONV_K - 1:
                            link(ins)
                    ins.then_inc(S("conv"), 1)
                for j in range(4):
                    dve.wait_ge(S("cfs"), j + 1)
                    dve.tensor_tensor(yc[:, j, :], bank[1 + (2 * j) % 4][:, :], sg_t, ALU.mult).then_inc(S("yc"), 1)
                    if j >= 1:
                        column_conv(j - 1)
                column_conv(3)
                dve.wait_ge(S("g_b"), 3)
                link(dve.tensor_tensor(g1, g1, g2, ALU.add))
                na = nal.rearrange("p (o d h) -> p o d h", o=1, d=2)
                for t in range(NT):
                    ins = dve.scalar_tensor_tensor(out=gg[:, t, :, :], in0=g1[:, t, :, :], scalar=-1.0, in1=na[:, 0, :, :],
                                                   op0=ALU.mult, op1=ALU.mult)
                ins.then_inc(S("gg"), 1)
                nsq = 0
                for t in range(NT):
                    nsq += 1
                    dve.wait_ge(S("sq"), nsq)
                    dve.tensor_reduce(ssq[:, 0:4], h4(lane[0]["et"]), AX.X, ALU.add)
                    if t >= NT_C:
                        nsq += 1
                        dve.wait_ge(S("sq"), nsq)
                        dve.tensor_reduce(ssq[:, 4:8], h4(lane[1]["et"]), AX.X, ALU.add).then_inc(S("ssq"), 1)
                    else:
                        dve.memset(ssq[:, 4:8], 1.0).then_inc(S("ssq"), 1)
                    dve.wait_ge(S("rq"), 2 * (t + 1))
                    link(dve.reciprocal(rq2, rq))
                    r3 = rq2.rearrange("p (a h o) -> p a h o", a=2, o=1)
                    ins = dve.tensor_tensor(h4(kn[:, t, :]), h4(bank[1][:, :]), bc(r3[:, 0, :, :], [P, 4, P]), ALU.mult)
                    if t >= NT_C:
                        ins = dve.tensor_tensor(h4(qn[:, t - NT_C, :]), h4(bank[0][:, :]), bc(r3[:, 1, :, :], [P, 4, P]), ALU.mult)
                    ins.then_inc(S("kqn"), 1)

                dve.memset(state.rearrange("p d c -> p (d c)"), 0.0).then_inc(S("state0"), 1)
                dve.wait_ge(S("masks"), 14)
                i4 = ident.rearrange("p (o c) -> p o c", o=1)
                for p in range(6):
                    both = [(l, d, t) for l, (d, t) in enumerate(PAIRS[p])]
                    for l, d, t in both:
                        B, L = bank[4 * l:4 * l + 4], lane[l]
                        dve.wait_ge(S(f"grow{l}"), p + 1)
                        last = (CHUNK - 1) if d == 0 else 0
                        if p >= 1:
                            dve.wait_ge(S(f"sg{l}"), 2 * p)
                        dve.tensor_copy(gl[l], h4(B[0][:, :])[:, :, last::CHUNK])
                        link(dve.tensor_copy(gcs[l], B[1][:, 0:4]), f"gc{l}")
                        g3 = gcs[l].rearrange("p (h o) -> p h o", o=1)
                        link(dve.tensor_tensor(h4(L["et"]), h4(B[0][:, :]), bc(g3, [P, 4, P]), ALU.subtract))
                        dve.tensor_scalar(L["et"], L["et"], 0.0, None, ALU.min).then_inc(S(f"dd{l}"), 1)
                        dve.wait_ge(S(f"ex{l}"), p + 1)
                        dve.wait_ge(S(f"gl{l}"), p + 1)
                        dve.tensor_tensor(h4(L["et"]), h4(L["lt"]), bc(upto[:, d:d + 1, :], [P, 4, P]), ALU.mult).then_inc(S(f"et{l}"), 1)
                        if p >= 1:
                            dve.wait_ge(S(f"kd{l}"), p)
                        for c in range(2):
                            r = slice(CHUNK * c, CHUNK * c + CHUNK)
                            i = CHUNK * c + last
                            ins = dve.tensor_copy(kdl[l][r], h4(L["lt"])[r, :, i:i + 1])
                        ins.then_inc(S(f"kdl{l}"), 1)
                    for l, d, t in both:
                        B, L = bank[4 * l:4 * l + 4], lane[l]
                        dve.wait_ge(S(f"lt_mm{l}"), p + 1)
                        dve.wait_ge(S(f"et{l}"), p + 1)
                        dve.tensor_tensor(L["lt"], B[0][:, :], L["et"], ALU.mult).then_inc(S(f"lt{l}"), 1)
                        dve.wait_ge(S(f"lt{l}"), p + 1)
                        link(dve.tensor_tensor(h4(L["y"]), h4(L["lt"]), bc(lvl[:, d, 0:1, :], [P, 4, P]), ALU.mult))
                        dve.tensor_tensor(h4(L["y"]), bc(i4, [P, 4, P]), h4(L["y"]), ALU.subtract).then_inc(S(f"y{l}"), 1)
                        if p >= 2:
                            dve.wait_ge(S(f"it_mm{l}"), p - 1)
                            dve.tensor_tensor(L["it"], B[1][:, :], L["et"], ALU.mult).then_inc(S(f"it{l}"), 1)
                    for n in range(5):
                        for l, d, t in both:
                            B, L = bank[4 * l:4 * l + 4], lane[l]
                            dve.wait_ge(S(f"xy_mm{l}"), 5 * p + n + 1)
                            if n < 4:
                                if n == 0:
                                    dve.wait_ge(S(f"x{l}"), 5 * p + 1)
                                dve.tensor_tensor(L["x"], L["x"], B[1][:, :], ALU.subtract).then_inc(S(f"x{l}"), 1)
                            dve.wait_ge(S(f"y{l}"), 6 * p + n + 1)
                            dve.tensor_tensor(L["y"], L["y"], B[2][:, :], ALU.subtract).then_inc(S(f"y{l}"), 1)
                    for j in range(2):
                        for l, d, t in both:
                            B, L = bank[4 * l:4 * l + 4], lane[l]
                            c = j if d == 0 else 1 - j
                            r = slice(CHUNK * c, CHUNK * c + CHUNK)
                            n = 2 * p + j
                            if n >= 1:
                                dve.wait_ge(S(f"scan_ev{l}"), n)
                            else:
                                dve.wait_ge(S("state0"), 1)
                            g3 = gl[l][:, :, c:c + 1]
                            dve.wait_ge(S(f"kbg{l}"), p + 1)
                            dve.tensor_tensor(h4(L["kb"]), h4(state[:, d, :]), bc(g3, [P, 4, P]), ALU.mult).then_inc(S(f"sg{l}"), 1)
                            dve.wait_ge(S(f"ws_mm{l}"), n + 1)
                            dve.wait_ge(S(f"uw{l}"), p + 1)
                            dve.tensor_tensor(L["vn"][r, :], L["u"][r, :], B[1][r, :], ALU.subtract).then_inc(S(f"vn{l}"), 1)
                        for l, d, t in both:
                            B, L = bank[4 * l:4 * l + 4], lane[l]
                            c = j if d == 0 else 1 - j
                            r = slice(CHUNK * c, CHUNK * c + CHUNK)
                            n = 2 * p + j
                            dve.wait_ge(S(f"su_mm{l}"), n + 1)
                            dve.wait_ge(S(f"sg{l}"), n + 1)
                            dve.tensor_tensor(state[:, d, :], L["kb"], B[2][:, :], ALU.add).then_inc(S(f"scan_ev{l}"), 1)
                            if p >= 4:
                                lo = 1 - l
                                dve.wait_ge(S(f"o_ev{lo}"), 4)
                                dve.tensor_tensor(o_acc[r, t - NT_C, :], o_acc[r, t - NT_C, :], B[3][r, :], ALU.add).then_inc(S(f"o_ev{l}"), 1)

                dve.wait_ge(S("osq"), 1)
                dve.tensor_reduce(so, sq4.rearrange("p (g c) -> p g c", c=P), AX.X, ALU.add).then_inc(S("ossq"), 1)
                dve.wait_ge(S("cf_sum"), 1)
                for j in range(4):
                    dve.scalar_tensor_tensor(out=cen[:, j, :], in0=bank[0][:, :], scalar=-1.0 / 512, in1=cv[:, j, :],
                                             op0=ALU.mult, op1=ALU.add).then_inc(S("cen"), 1)
                dve.wait_ge(S("orq"), 1)
                link(dve.reciprocal(so2, so))
                dve.tensor_tensor(onr.rearrange("p (g c) -> p g c", c=P), o_acc.rearrange("p t (h c) -> p (t h) c", c=P),
                                  bc(so2.rearrange("p (g o) -> p g o", o=1), [P, 16, P]), ALU.mult).then_inc(S("onr"), 1)
                for h in range(HEADS):
                    dve.wait_ge(S("hd_mm"), h + 1)
                    dve.scalar_tensor_tensor(out=heads[:, h, :], in0=bank[2 + h][:, :], scalar=col("dn_norm_g"), in1=sz[:, h, :],
                                             op0=ALU.mult, op1=ALU.mult).then_inc(S("hd"), 1)
                dve.wait_ge(S("cf_rt"), 1)
                link(dve.reciprocal(rst, rst))
                for j in range(4):
                    dve.tensor_tensor(cen[:, j, :], cen[:, j, :], rst, ALU.mult).then_inc(S("cfn"), 1)
                dve.wait_ge(S("cfn"), 4)
                dve.engine_nop().then_inc(S("rstd_used"), 1)
                dve.wait_ge(S("xr_in"), 16)
                for n in range(8):
                    half, t = n // 4, n % 4
                    dve.wait_ge(S("wo_mm"), n + 1)
                    cs_ = slice(512 * half, 512 * half + 512)
                    if n >= 2:
                        dve.wait_ge(S("xmid"), n - 1)
                    link(dve.tensor_tensor(gtmp[n % 2], bank[n][:, :], modrow[:, 0, cs_], ALU.mult))
                    dve.tensor_tensor(xr[:, t, cs_], xr[:, t, cs_], gtmp[n % 2], ALU.add).then_inc(S("xmid"), 1)

            @block.gpsimd
            def _(pool):
                pool.memset(ident, 0.0)
                pool.memset(ones, 1.0)
                pool.memset(upto.rearrange("p d c -> p (d c)"), 1.0)
                pool.memset(lvl.rearrange("p d l c -> p (d l c)"), 1.0).then_inc(S("ident"), 1)
                pool.wait_ge(S("ident"), 1)
                pool.affine_select(out=ident, in_=ident, compare_op=ALU.not_equal, fill=1.0, base=0, pattern=[[-1, P]],
                                   channel_multiplier=1).then_inc(S("ident"), 1)
                nm = [0]

                def keep(ap, op, base, pattern, cm):
                    pool.affine_select(out=ap, in_=ap, compare_op=op, fill=0.0, base=base, pattern=pattern,
                                       channel_multiplier=cm).then_inc(S("mk"), 1)
                    nm[0] += 1
                    pool.wait_ge(S("mk"), nm[0])
                for d in range(2):
                    sgn = 1 if d == 0 else -1
                    m = upto[:, d, :]
                    keep(m, ALU.is_ge, 0, [[sgn, P]], -sgn)
                    v = m.rearrange("p (b c) -> p b c", c=CHUNK)
                    keep(v, ALU.is_ge, 0, [[-CHUNK, 2], [0, CHUNK]], 1)
                    keep(v, ALU.is_ge, CHUNK - 1, [[CHUNK, 2], [0, CHUNK]], -1)
                    pool.sem_inc(S("masks"), 1)
                    for l, s in enumerate([1] + LEVELS):
                        m = lvl[:, d, l, :]
                        nb = P // (2 * s)
                        v = m.rearrange("p (b u c) -> p b u c", u=2, c=s)
                        lo, hi = (0, s - 1) if d == 0 else (s, 2 * s - 1)
                        keep(v, ALU.is_ge, -lo, [[-2 * s, nb], [0, 2], [0, s]], 1)
                        keep(v, ALU.is_ge, hi, [[2 * s, nb], [0, 2], [0, s]], -1)
                        if d == 0:
                            keep(v, ALU.is_ge, -1, [[0, nb], [1, 2], [0, s]], 0)
                        else:
                            keep(v, ALU.is_ge, 0, [[0, nb], [-1, 2], [0, s]], 0)
                        pool.sem_inc(S("masks"), 1)
                pool.wait_ge(S("gg"), 1)
                pool.wait_ge(S("beta"), 1)
                pool.wait_ge(S("kqT"), NT)
                pool.wait_ge(S("vt"), NT)
                for p in range(6):
                    both = [(l, d, t) for l, (d, t) in enumerate(PAIRS[p])]
                    for l, d, t in both:
                        B, L = bank[4 * l:4 * l + 4], lane[l]
                        if p >= 1:
                            pool.wait_ge(S(f"uw_mm{l}"), p)
                        pool.tensor_tensor(h4(L["ct"]), bc(upto[:, d:d + 1, :], [P, 4, P]),
                                           bc(gg[:, t, d, :].rearrange("p (h o) -> p h o", o=1), [P, 4, P]), ALU.mult).then_inc(S(f"ug{l}"), 1)
                        b3 = bc(beta[:, t, d, :].rearrange("p (h o) -> p h o", o=1), [P, 4, P])
                        if p >= 1:
                            pool.wait_ge(S(f"scan_ev{l}"), 2 * p)
                        pool.tensor_tensor(h4(L["kb"]), h4(kn[:, t, :]), b3, ALU.mult).then_inc(S(f"kb{l}"), 1)
                        pool.tensor_tensor(h4(L["vb"]), h4(vt[:, t, :]), b3, ALU.mult)
                        if p >= 1:
                            pool.wait_ge(S(f"scan_ev{l}"), 2 * p)
                        pool.wait_ge(S(f"eg{l}"), p + 1)
                        e3 = bc(eg[l].rearrange("p (h o) -> p h o", o=1), [P, 4, P])
                        if p >= 2:
                            pool.tensor_tensor(h4(L["u"]), h4(qn[:, t - NT_C, :]), e3, ALU.mult).then_inc(S(f"qd{l}"), 1)
                        pool.wait_ge(S(f"kb{l}"), p + 1)
                        pool.tensor_tensor(h4(L["kbg"]), h4(L["kb"]), e3, ALU.mult).then_inc(S(f"kbg{l}"), 1)
                        pool.wait_ge(S(f"kdl{l}"), p + 1)
                        pool.tensor_tensor(h4(L["kd"]), h4(kn[:, t, :]), bc(kdl[l], [P, 4, P]), ALU.mult).then_inc(S(f"kd{l}"), 1)
                    for n in range(5):
                        for l, d, t in both:
                            L = lane[l]
                            pool.wait_ge(S(f"lt{l}"), p + 1)
                            if n >= 1:
                                pool.wait_ge(S(f"t1_mm{l}"), 5 * p + n)
                            pool.tensor_tensor(h4(L["ct"]), h4(L["lt"]), bc(lvl[:, d, n + 1:n + 2, :], [P, 4, P]), ALU.mult).then_inc(S(f"ct{l}"), 1)

        end_phase()
        NCOL = 96
        ITEM_RING = 3
        BASE_GROUPS = N_EXP // ITEM_RING + 1
        GUW = KD * 2 * F_EXP
        slot = [at(EXPW * i, EXPW) for i in range(ITEM_RING)]
        w_sh = at(RING * WCH + KD * (T_C + T_X), EXPW)
        xg = [at(24576 + D * i, D) for i in range(ITEM_RING)]
        MB = TB + N_COLS2
        xgT = [at(MB + D * i, D).rearrange("p (k c) -> p k c", k=KD) for i in range(ITEM_RING)]
        sgl = at(MB, 1024).rearrange("p (m c) -> p m c", m=2)
        hs = at(MB + 1024, 1024).rearrange("p (m c) -> p m c", m=2)
        oh = at(MB + 3072, 512).rearrange("p (t c) -> p t c", t=NT_X)
        ag = at(MB + 3584, F_EXP)
        aa = at(MB + 3840, F_EXP)
        aT = at(MB + 4096, F_EXP).rearrange("p (m c) -> p m c", m=2)
        yb = [at(24576 + 3108 + 4096 + D * i, D) for i in range(ITEM_RING)]
        posx = at(MB + 4352, 4 * NCOL).rearrange("p (t n) -> p t n", t=NT_X)
        iof = at(MB + 4736, P)
        ei = at(MB + 4864, NCOL).bitcast(I32)
        io_i = at(MB + 4960, P).bitcast(I32)
        cnt_i = at(MB + 5088, 2).bitcast(I32)
        idx = [at(MB + 5090 + 2 * i, 2).bitcast(U32) for i in range(ITEM_RING)]
        wsl = [at(MB + 5096 + i, 1) for i in range(ITEM_RING)]
        sidx = [at(MB + 5150 + i, 1).bitcast(U32) for i in range(ITEM_RING)]
        ve = at(MB + 5100, 16).rearrange("p (t v) -> p t v", t=NT_X)
        tokf = at(MB + 5116, 4)
        tok6 = at(MB + 5120, 4)
        jp = at(MB + 5124, 1)
        jp1 = at(MB + 5125, 1)
        tk_i = at(MB + 5126, 4).bitcast(I32)
        hss, hrt, hrs = at(MB + 5130, 4), at(MB + 5134, 4), at(MB + 5138, 4)
        vx = lvl.rearrange("p d l c -> p (d l c)").rearrange("p (t n v) -> p t n v", t=NT_X, v=4)
        tri = upto[:, 0, :]
        rbias = upto[:, 1, 0:N_EXP]
        RT = tmpA
        ra = [at(RT + 256 * i, 256) for i in range(20)]
        rsm = [at(RT + 5120 + 32 * i, 32) for i in range(32)]
        sqj = [at(tmpA + D * i, D) for i in range(2)]
        BIG = 1.0e30

        def w(eng, name, val):
            if val is None or isinstance(val, int) and val <= 0:
                return
            eng.wait_ge(S(name), val)

        def groups(eng, body):
            w(eng, "plan", 1)
            n = eng.value_load(cnt_i[0:1, 0:1], min_val=0, max_val=8) + BASE_GROUPS
            body(0)
            body(1)
            with eng.Fori(2, n) as i:
                body(i)
            return n

        def load_moe(sp):
            sp.dma_start(gffn, a["rows"][ROWS["g_ffn"][0]:ROWS["g_ffn"][0] + D].partition_broadcast(P)).then_inc(S("gffn_in"), 16)
            sp.dma_start(cols2, a["cols2"]).then_inc(S("cols2_in"), 16)
            sp.dma_start(w_sh, a["wsh"]).then_inc(S("wsh_in"), 16)
            sp.dma_start(rbias, a["rows"][16:16 + N_EXP].partition_broadcast(P)).then_inc(S("rb_in"), 16)
            for t in range(NT_X):
                sp.wait_ge(S("h2"), t + 1)
                sp.dma_start(h2d[t * P:(t + 1) * P, :], h2[:, t, :]).then_inc(S("h2_out"), 16)

            def item(i, s):
                n = i * ITEM_RING + s
                e = n if isinstance(n, int) else sp.value_load(ei[0:1, bass.ds(n, 1)], min_val=0, max_val=N_EXP - 1)
                src = a["wexp"][e] if isinstance(n, int) else a["wexp"][bass.ds(e, 1), :, :].rearrange("o p c -> p (o c)")
                w(sp, "gu_mm", n - 2)
                sp.dma_start(slot[s][:, 0:GUW], src[:, 0:GUW]).then_inc(S(f"wg{s}"), 16)
                w(sp, "dn_mm", n - 2)
                sp.dma_start(slot[s][:, GUW:], src[:, GUW:]).then_inc(S(f"wd{s}"), 16)

            def body(i):
                for s in range(ITEM_RING):
                    item(i, s)
            item(0, 0)
            item(0, 1)
            sp.wait_ge(S("plan"), 1)
            item(0, 2)
            n = sp.value_load(cnt_i[0:1, 0:1], min_val=0, max_val=8) + BASE_GROUPS
            with sp.Fori(1, n) as i:
                body(i)
            for t in range(NT_X):
                if t == 0:
                    sp.wait_ge(S("scattered"), 1)
                    sp.wait_ge(S("moe_pe"), 1)
                if t >= ITEM_RING:
                    sp.wait_ge(S("comb"), t - ITEM_RING + 1)
                sp.dma_start(slot[t % ITEM_RING], yd[t * P * TOP_K:(t + 1) * P * TOP_K, :].rearrange("(p k) d -> p (k d)", k=TOP_K)).then_inc(S(f"yd_in{t % ITEM_RING}"), 16)

        def moe_pe(pe):
            for k in range(KD):
                if k == 0:
                    pe.wait_ge(S("h2"), 4)
                if k >= 4:
                    pe.wait_ge(S("h2T"), k - 3)
                for t in range(NT_X):
                    mm = pe.transpose(bank[k % 4][:, t * P:(t + 1) * P], h2[:, t, k * P:(k + 1) * P], ident)
                mm.then_inc(S("h2T_mm"), 1)
            pe.wait_ge(S("h2T"), KD)
            pe.wait_ge(S("cols2_in"), 16)
            rw = col2("router_w", 0, KD * N_EXP).rearrange("p (k c) -> p k c", k=KD)
            for t in range(NT_X):
                for k in range(KD):
                    mm = pe.matmul(bank[4][:, t * N_EXP:(t + 1) * N_EXP], h2T[:, k, t * P:(t + 1) * P], rw[:, k, :],
                                   start=(k == 0), stop=(k == KD - 1))
            mm.then_inc(S("lg_mm"), 1)
            pe.wait_ge(S("wsh_in"), 16)
            wg = w_sh[:, 0:GUW].rearrange("p (k c) -> p k c", k=KD)
            for m in (0, 2, 1, 3):
                for k in range(KD):
                    mm = pe.matmul(bank[m][:, :], wg[:, k, m * P:(m + 1) * P], h2T[:, k, :], start=(k == 0), stop=(k == KD - 1))
                mm.then_inc(S("sgu_mm"), 1)
            pe.wait_ge(S("mask"), 1)
            pe.wait_ge(S("tri"), 1)
            pe.wait_ge(S("th"), 1)
            for t in range(NT_X):
                for t2 in range(t):
                    pe.matmul(bank[4][:, t * N_EXP:(t + 1) * N_EXP], ones, ra[8][:, t2 * N_EXP:(t2 + 1) * N_EXP],
                              start=(t2 == 0), stop=False)
                pe.matmul(bank[4][:, t * N_EXP:(t + 1) * N_EXP], tri, ra[8][:, t * N_EXP:(t + 1) * N_EXP],
                          start=(t == 0), stop=True)
            for t in range(NT_X):
                mm = pe.matmul(bank[4][:, 256:256 + N_EXP], ones, ra[8][:, t * N_EXP:(t + 1) * N_EXP], start=(t == 0), stop=(t == 3))
            mm.then_inc(S("cum_mm"), 1)
            pe.wait_ge(S("hs"), 2)
            pe.wait_ge(S("over"), 1)
            pe.transpose(bank[0][0:N_EXP, 0:P], ra[12][:, 0:N_EXP], ident)
            pe.matmul(bank[0][:, 128:256], ra[13][:, 0:P], ident, start=True, stop=True)
            mm = pe.matmul(bank[0][:, 256:384], ra[13][:, P:2 * P], ident, start=True, stop=True)
            mm.then_inc(S("tr_mm"), 1)
            for c, arr in enumerate((posx[:, :, 0:N_EXP], vx[:, :, 0:N_EXP, 1], vx[:, :, 0:N_EXP, 2])):
                for t in range(NT_X):
                    mm = pe.transpose(bank[1 + c][0:N_EXP, t * P:(t + 1) * P], arr[:, t, :], ident)
            mm.then_inc(S("tr_mm"), 1)
            wd = w_sh[:, GUW:].rearrange("p (k c) -> p k c", k=2)
            for u in range(8):
                t, half = u // 2, u % 2
                if u >= 3:
                    pe.wait_ge(S("shx"), u - 2)
                for k in range(2):
                    mm = pe.matmul(bank[5 + u % 3][:, :], hs[:, k, t * P:(t + 1) * P], wd[:, k, half * 512:half * 512 + 512],
                                   start=(k == 0), stop=(k == 1))
                mm.then_inc(S("sdn_mm"), 1)
            pe.wait_ge(S("trc"), 4)
            for c in range(3):
                for t in range(NT_X):
                    mm = pe.matmul(bank[4][:, (c * 4 + t) * 32:(c * 4 + t + 1) * 32], trT[c][0:N_EXP, t * P:(t + 1) * P],
                                   selT[0:N_EXP, 0:32], start=True, stop=True)
            mm.then_inc(S("sel_mm"), 1)
            pe.wait_ge(S("plan"), 1)
            pe.wait_ge(S("shx"), 8)

            def index(n):
                w(pe, "oh", n + 1)
                w(pe, "idx", n)
                for t in range(NT_X):
                    mm = pe.matmul(bank[0][:, 0:4], oh[:, t, :], ve[:, t, :], start=(t == 0), stop=(t == NT_X - 1))
                mm.then_inc(S("ix_mm"), 1)

            def turn(n, s, i):
                w(pe, f"gat{s}", 16 * (i + 1))
                w(pe, "xgT", 2 * n)
                for k in range(KD):
                    mm = pe.transpose(bank[1 + k // 4][:, (k % 4) * P:(k % 4 + 1) * P], xg[s][:, k * P:(k + 1) * P], ident)
                    if k % 4 == 3:
                        mm.then_inc(S("xt_mm"), 1)

            def down(n, s, i):
                w(pe, "aT", n + 1)
                w(pe, f"wd{s}", 16 * (i + 1))
                w(pe, "y", n)
                w(pe, "yy", n)
                wv = slot[s][:, GUW:].rearrange("p (k c) -> p k c", k=2)
                for half in range(2):
                    for k in range(2):
                        mm = pe.matmul(bank[5 + half][:, :], aT[:, k, :], wv[:, k, half * 512:half * 512 + 512],
                                       start=(k == 0), stop=(k == 1))
                mm.then_inc(S("dn_mm"), 1)

            def body(i):
                for s in range(ITEM_RING):
                    n = i * ITEM_RING + s
                    w(pe, "xgT", 2 * n + 1)
                    w(pe, f"wg{s}", 16 * (i + 1))
                    w(pe, "aa", n)
                    wv = slot[s][:, 0:GUW].rearrange("p (k c) -> p k c", k=KD)
                    for k in range(KD):
                        if k == 4:
                            w(pe, "xgT", 2 * (n + 1))
                        mm = pe.matmul(bank[3][:, :], xgT[s][:, k, :], wv[:, k, :], start=(k == 0), stop=(k == KD - 1))
                    mm.then_inc(S("gu_mm"), 1)
                    if not (isinstance(n, int) and n == 0):
                        down(n - 1, (s - 1) % ITEM_RING, i if s else i - 1)
                    index(n + 2)
                    turn(n + 1, (s + 1) % ITEM_RING, i if s < 2 else i + 1)
                    w(pe, "aa", n + 1)
                    w(pe, "aT", n)
                    for m in range(2):
                        mm = pe.transpose(bank[4][:, m * P:(m + 1) * P], aa[:, m * P:(m + 1) * P], ident)
                    mm.then_inc(S("at_mm"), 1)
            index(0)
            index(1)
            turn(0, 0, 0)
            n = groups(pe, body)
            down(n * ITEM_RING - 1, ITEM_RING - 1, n - 1)
            pe.wait_ge(S("y"), n * ITEM_RING)
            pe.wait_ge(S("yy"), n * ITEM_RING)
            pe.sem_inc(S("moe_pe"), 1)

        trT = [at(RT + 256 * 14 + 512 * i, 512) for i in range(3)]
        selT = ra[6]

        def moe_act(act):
            for t in range(NT_X):
                if t >= 2:
                    act.wait_ge(S("hss"), t - 1)
                act.activation(sqj[t % 2], xr[:, t, :], ACT.Square, accum_out=hss[:, t:t + 1]).then_inc(S("hss"), 1)
            act.wait_ge(S("hss"), 4)
            act.activation(hrt, hss, ACT.Sqrt, scale=1.0 / D, bias=eps1).then_inc(S("hrt"), 1)
            for k in range(KD):
                act.wait_ge(S("h2T_mm"), k + 1)
                act.activation(h2T[:, k, :], bank[k % 4][:, :], ACT.Copy).then_inc(S("h2T"), 1)
            act.wait_ge(S("lg_mm"), 1)
            act.wait_ge(S("hrt"), 1)
            act.activation(ra[0], bank[4][:, 0:256], ACT.Tanh, scale=0.5).then_inc(S("th"), 1)
            for m in range(2):
                act.wait_ge(S("sgu_mm"), 2 * m + 1)
                act.activation(sgl[:, m, :], bank[m][:, :], ACT.Silu).then_inc(S("sgl"), 1)

            def widen(n, s):
                for c in range(2):
                    w(act, "xt_mm", 2 * n + c + 1)
                    act.activation(xgT[s][:, 4 * c:4 * c + 4, :], bank[1 + c][:, :].rearrange("p (k c) -> p k c", k=4), ACT.Copy).then_inc(S("xgT"), 1)

            def out(n, s, i):
                w(act, "dn_mm", n + 1)
                w(act, f"ys{s}", 16 * i)
                act.activation(yb[s][:, 0:512], bank[5][:, :], ACT.Copy, scale=wsl[s]).then_inc(S("y"), 1)

            def body(i):
                for s in range(ITEM_RING):
                    n = i * ITEM_RING + s
                    w(act, "gu_mm", n + 1)
                    act.activation(ag, bank[3][:, 0:F_EXP], ACT.Silu).then_inc(S("ag"), 1)
                    if not (isinstance(n, int) and n == 0):
                        out(n - 1, (s - 1) % ITEM_RING, i if s else i - 1)
                    widen(n + 1, (s + 1) % ITEM_RING)
            act.wait_ge(S("sdn_mm"), 8)
            act.wait_ge(S("hs"), 2)
            widen(0, 0)
            n = groups(act, body)
            out(n * ITEM_RING - 1, ITEM_RING - 1, n - 1)

        def moe_dve(dve):
            count = {}

            def link(ins, signal="dve_route"):
                count[signal] = count.get(signal, 0) + 1
                ins.then_inc(S(signal), 1)
                dve.wait_ge(S(signal), count[signal])

            dve.wait_ge(S("gffn_in"), 16)
            link(dve.tensor_scalar(modrow[:, 2, :], modrow[:, 2, :], 1.0, None, ALU.add))
            link(dve.tensor_tensor(modrow[:, 2, :], modrow[:, 2, :], gffn, ALU.mult))
            dve.wait_ge(S("hrt"), 1)
            link(dve.reciprocal(hrs, hrt))
            for t in range(NT_X):
                link(dve.scalar_tensor_tensor(out=h2[:, t, :], in0=xr[:, t, :], scalar=hrs[:, t:t + 1], in1=modrow[:, 2, :],
                                              op0=ALU.mult, op1=ALU.mult))
                dve.tensor_tensor(h2[:, t, :], h2[:, t, :], modrow[:, 1, :], ALU.add).then_inc(S("h2"), 1)
            dve.wait_ge(S("iota"), 1)
            dve.tensor_copy(iof, io_i)
            dve.tensor_copy(tokf, tk_i)
            link(dve.tensor_copy(jp, tk_i[:, 0:1]))
            dve.tensor_scalar(jp1, jp, 1.0, None, ALU.add)
            link(dve.tensor_scalar(tok6, tokf, float(TOP_K), -1.0 - 4096.0, ALU.mult, ALU.add))
            link(dve.tensor_scalar(tokf, tokf, -4096.0, None, ALU.add))
            seg64, seg8 = ra[1], rsm[0]
            dve.memset(seg64, 1.0)
            link(dve.memset(seg8, 1.0))
            dve.memset(seg64.rearrange("p (t e) -> p t e", t=4)[:, :, 0:1], 0.0)
            link(dve.memset(seg8.rearrange("p (t e) -> p t e", t=4)[:, :, 0:1], 0.0))

            def v4(ap):
                return ap.rearrange("p (t e) -> p t e", t=4)

            def choose(val, m8, k, seg, gt, eq, cnt, cum, n):
                thr = m8.rearrange("p (t e) -> p t e", t=4)[:, :, k - 1:k]
                dve.tensor_tensor(v4(gt), v4(val), bc(thr, [P, 4, n]), ALU.is_gt)
                link(dve.tensor_tensor(v4(eq), v4(val), bc(thr, [P, 4, n]), ALU.is_equal))
                dve.tensor_reduce(cnt, v4(gt), AX.X, ALU.add)
                link(dve.tensor_tensor_scan(cum, seg, eq, 0.0, ALU.mult, ALU.add))
                link(dve.tensor_tensor(v4(cum), v4(cum), bc(cnt.rearrange("p (t o) -> p t o", o=1), [P, 4, n]), ALU.add))
                link(dve.scalar_tensor_tensor(out=cum, in0=cum, scalar=float(k), in1=eq, op0=ALU.is_le, op1=ALU.mult))
                link(dve.tensor_tensor(gt, gt, cum, ALU.add))

            sc, sel = ra[2], ra[3]
            dve.wait_ge(S("th"), 1)
            dve.wait_ge(S("rb_in"), 16)
            link(dve.tensor_scalar(sc, ra[0], 0.5, 0.5, ALU.mult, ALU.add))
            link(dve.tensor_tensor(v4(sel), v4(sc), bc(rbias.rearrange("p (o e) -> p o e", o=1), [P, 4, N_EXP]), ALU.add))
            m8 = ra[4].rearrange("p (g e) -> p g e", e=8)
            for g in range(32):
                ins = dve.max(m8[:, g, :], sel[:, 8 * g:8 * g + 8])
            link(ins)
            gs = rsm[1]
            link(dve.tensor_tensor(gs, m8[:, :, 0], m8[:, :, 1], ALU.add))
            for t in range(4):
                ins = dve.max(rsm[2][:, 8 * t:8 * t + 8], gs[:, 8 * t:8 * t + 8])
            link(ins)
            choose(gs, rsm[2], KEEP_GRP, seg8, rsm[3], rsm[4], rsm[5][:, 0:4], rsm[6], 8)
            link(dve.tensor_scalar(rsm[7], rsm[3], BIG, -BIG, ALU.mult, ALU.add))
            g8v = lambda ap: ap.rearrange("p (g e) -> p g e", e=8)
            link(dve.tensor_tensor(g8v(ra[5]), g8v(sel), bc(rsm[3].rearrange("p (g o) -> p g o", o=1), [P, 32, 8]), ALU.mult))
            link(dve.tensor_tensor(g8v(ra[5]), g8v(ra[5]), bc(rsm[7].rearrange("p (g o) -> p g o", o=1), [P, 32, 8]), ALU.add))
            for t in range(4):
                ins = dve.max(rsm[8][:, 8 * t:8 * t + 8], ra[5][:, 64 * t:64 * t + 64])
            link(ins)
            choose(ra[5], rsm[8], TOP_K, seg64, ra[8], ra[7], rsm[9][:, 0:4], ra[9], N_EXP)
            mask = ra[8]
            dve.engine_nop().then_inc(S("mask"), 1)
            link(dve.tensor_tensor(ra[10], sc, mask, ALU.mult))
            dve.tensor_reduce(rsm[10][:, 0:4], v4(ra[10]), AX.X, ALU.add)
            link(dve.tensor_tensor_scan(ra[11], seg64, mask, 0.0, ALU.mult, ALU.add))
            link(dve.reciprocal(rsm[11][:, 0:4], rsm[10][:, 0:4]))
            link(dve.tensor_scalar(rsm[11][:, 0:4], rsm[11][:, 0:4], ROUTED_SCALE, None, ALU.mult))
            dve.memset(vx.rearrange("p t n v -> p (t n v)"), 0.0).then_inc(S("vx0"), 1)
            dve.wait_ge(S("vx0"), 1)
            c3 = lambda ap: ap.rearrange("p (t o) -> p t o", o=1)
            dve.tensor_tensor(vx[:, :, 0:N_EXP, 2], v4(ra[10]), bc(c3(rsm[11][:, 0:4]), [P, 4, N_EXP]), ALU.mult)
            dve.tensor_tensor(vx[:, :, 0:N_EXP, 1], v4(ra[11]), bc(c3(tok6), [P, 4, N_EXP]), ALU.add)
            link(dve.tensor_tensor(vx[:, :, :, 0], vx[:, :, :, 0], bc(c3(tokf), [P, 4, NCOL]), ALU.add))
            for m in range(2):
                dve.wait_ge(S("sgl"), m + 1)
                dve.wait_ge(S("sgu_mm"), 2 * m + 2)
                dve.tensor_tensor(hs[:, m, :], sgl[:, m, :], bank[2 + m][:, :], ALU.mult).then_inc(S("hs"), 1)
            dve.wait_ge(S("cum_mm"), 1)
            link(dve.tensor_tensor(posx[:, :, 0:N_EXP], v4(bank[4][:, 0:256]), v4(mask), ALU.mult))
            dve.tensor_scalar(posx[:, :, 0:N_EXP], posx[:, :, 0:N_EXP], -1.0, None, ALU.add)
            tot, nb, incl, excl, M = ra[12][:, 64:128], ra[12][:, 128:192], ra[9][:, 0:64], ra[9][:, 64:128], ra[12][:, 0:64]
            link(dve.tensor_copy(tot, bank[4][:, 256:256 + N_EXP]))
            link(dve.tensor_scalar(nb, tot, 128.5, None, ALU.is_gt))
            link(dve.scalar_tensor_tensor(out=nb, in0=tot, scalar=256.5, in1=nb, op0=ALU.is_gt, op1=ALU.add))
            link(dve.scalar_tensor_tensor(out=nb, in0=tot, scalar=384.5, in1=nb, op0=ALU.is_gt, op1=ALU.add))
            link(dve.memset(ra[9][:, 128:192], 1.0))
            link(dve.tensor_tensor_scan(incl, ra[9][:, 128:192], nb, 0.0, ALU.mult, ALU.add))
            link(dve.tensor_tensor(excl, incl, nb, ALU.subtract))
            link(dve.tensor_scalar(nb, excl, jp, None, ALU.is_le))
            link(dve.scalar_tensor_tensor(out=M, in0=incl, scalar=jp, in1=nb, op0=ALU.is_gt, op1=ALU.mult))
            dve.tensor_reduce(rsm[12][:, 0:1], M, AX.X, ALU.add)
            dve.tensor_tensor(tot, M, iof[:, 0:N_EXP], ALU.mult)
            link(dve.tensor_scalar(nb, excl, -1.0, jp1, ALU.mult, ALU.add))
            link(dve.tensor_tensor(nb, nb, M, ALU.mult))
            dve.tensor_reduce(rsm[12][:, 1:2], tot, AX.X, ALU.add)
            link(dve.tensor_reduce(rsm[12][:, 2:3], nb, AX.X, ALU.add))
            link(dve.tensor_scalar(rsm[12][:, 0:1], rsm[12][:, 0:1], -9.0, 9.0, ALU.mult, ALU.add))
            link(dve.tensor_tensor(rsm[12][:, 2:3], rsm[12][:, 2:3], rsm[12][:, 0:1], ALU.add))
            link(dve.tensor_scalar(rsm[12][:, 2:3], rsm[12][:, 2:3], -128.0, None, ALU.mult))
            dve.tensor_copy(ra[13][:, 0:P], bc(rsm[12][:, 1:2], [P, P]))
            link(dve.tensor_copy(ra[13][:, P:2 * P], bc(rsm[12][:, 2:3], [P, P])), "over")
            link(dve.tensor_scalar(rsm[13][:, 0:8], iof[:, 0:8], 3.0, 2.0, ALU.mult, ALU.add))
            link(dve.tensor_scalar(rsm[13][:, 0:8], rsm[13][:, 0:8], incl[:, 63:64], None, ALU.is_lt))
            link(dve.tensor_reduce(rsm[13][:, 8:9], rsm[13][:, 0:8], AX.X, ALU.add))
            dve.tensor_copy(cnt_i[:, 0:1], rsm[13][:, 8:9])
            dve.tensor_copy(ei[:, 0:N_EXP], io_i[:, 0:N_EXP])
            dve.wait_ge(S("tr_mm"), 1)
            dve.tensor_copy(ei[:, N_EXP:NCOL], bank[0][:, 128:160])
            dve.tensor_copy(rsm[14], bank[0][:, 256:288])
            link(dve.tensor_copy(selT[0:N_EXP, 0:P], bank[0][0:N_EXP, 0:P]), "trc")
            dve.wait_ge(S("tr_mm"), 2)
            for c in range(3):
                dve.tensor_copy(trT[c][0:N_EXP, :], bank[1 + c][0:N_EXP, :]).then_inc(S("trc"), 1)
            for u in range(8):
                t, half = u // 2, u % 2
                c_ = slice(half * 512, half * 512 + 512)
                dve.wait_ge(S("sdn_mm"), u + 1)
                if u >= 1:
                    dve.wait_ge(S("shx2"), u)
                dve.tensor_tensor(xg[0][:, 0:512], bank[5 + u % 3][:, :], modrow[:, 3, c_], ALU.mult).then_inc(S("shx"), 1)
                dve.wait_ge(S("shx"), u + 1)
                dve.tensor_tensor(xr[:, t, c_], xr[:, t, c_], xg[0][:, 0:512], ALU.add).then_inc(S("shx2"), 1)
            dve.wait_ge(S("shx2"), 8)
            for s in range(ITEM_RING):
                ins = dve.memset(xg[s], 0.0)
            ins.then_inc(S("xg0"), 1)
            dve.wait_ge(S("sel_mm"), 1)
            sv = bank[4][:, 0:384].rearrange("p (c t n) -> p c t n", c=3, t=4)
            dve.tensor_tensor(posx[:, :, N_EXP:NCOL], sv[:, 0], bc(rsm[14].rearrange("p (o n) -> p o n", o=1), [P, 4, 32]), ALU.add)
            dve.tensor_copy(vx[:, :, N_EXP:NCOL, 1], sv[:, 1])
            dve.tensor_copy(vx[:, :, N_EXP:NCOL, 2], sv[:, 2]).then_inc(S("plan"), 1)
            dve.wait_ge(S("plan"), 1)

            def onehot(n):
                w(dve, "ix_mm", n)
                sl = slice(n, n + 1) if isinstance(n, int) else bass.ds(n, 1)
                dve.tensor_copy(ve, vx[:, :, sl, :].rearrange("p t o v -> p t (o v)"))
                dve.tensor_tensor(oh, bc(iof.rearrange("p (o c) -> p o c", o=1), [P, 4, P]), bc(posx[:, :, sl], [P, 4, P]),
                                  ALU.is_equal).then_inc(S("oh"), 1)

            def index(n, s, behind):
                w(dve, "ix_mm", n + 1)
                w(dve, "y", behind)
                w(dve, "yy", behind)
                dve.tensor_scalar(idx[s], bank[0][:, 0:2], 4096.0, None, ALU.add)
                dve.tensor_copy(wsl[s], bank[0][:, 2:3]).then_inc(S("idx"), 1)

            def out(n, s, i):
                w(dve, "dn_mm", n + 1)
                w(dve, f"ys{s}", 16 * i)
                dve.tensor_copy(sidx[s], idx[s][:, 1:2])
                dve.tensor_scalar(yb[s][:, 512:1024], bank[6][:, :], wsl[s], None, ALU.mult).then_inc(S("yy"), 1)

            def body(i):
                for s in range(ITEM_RING):
                    n = i * ITEM_RING + s
                    onehot(n + 2)
                    w(dve, "ag", n + 1)
                    w(dve, "at_mm", n)
                    dve.tensor_tensor(aa, ag, bank[3][:, F_EXP:2 * F_EXP], ALU.mult).then_inc(S("aa"), 1)
                    if not (isinstance(n, int) and n == 0):
                        out(n - 1, (s - 1) % ITEM_RING, i if s else i - 1)
                    index(n + 2, (s + 2) % ITEM_RING, n)
                    w(dve, "at_mm", n + 1)
                    w(dve, "dn_mm", n)
                    dve.tensor_copy(aT, bank[4][:, 0:F_EXP].rearrange("p (m c) -> p m c", m=2)).then_inc(S("aT"), 1)
            onehot(0)
            index(0, 0, 0)
            onehot(1)
            index(1, 1, 0)
            n = groups(dve, body)
            out(n * ITEM_RING - 1, ITEM_RING - 1, n - 1)
            for t in range(NT_X):
                dve.wait_ge(S(f"yd_in{t % ITEM_RING}"), 16 * (t // ITEM_RING + 1))
                if t >= 1:
                    dve.wait_ge(S("combined"), 2 * t)
                red = xgT[0].rearrange("p k c -> p (k c)")
                dve.tensor_reduce(red, slot[t % ITEM_RING].rearrange("p (k d) -> p d k", k=TOP_K), AX.X, ALU.add).then_inc(S("comb"), 1)
                dve.wait_ge(S("comb"), t + 1)
                dve.tensor_tensor(red, red, modrow[:, 3, :], ALU.mult).then_inc(S("combined"), 1)
                dve.wait_ge(S("combined"), 2 * t + 1)
                dve.tensor_tensor(xr[:, t, :], xr[:, t, :], red, ALU.add).then_inc(S("combined"), 1)

        def moe_pool(pool):
            pool.iota(io_i, pattern=[[1, P]], base=0, channel_multiplier=0)
            pool.iota(tk_i, pattern=[[P, 4]], base=0, channel_multiplier=1).then_inc(S("iota"), 1)
            pool.memset(tri, 1.0).then_inc(S("tri0"), 1)
            pool.wait_ge(S("tri0"), 1)
            pool.affine_select(out=tri, in_=tri, compare_op=ALU.is_ge, fill=0.0, base=0, pattern=[[1, P]],
                               channel_multiplier=-1).then_inc(S("tri"), 1)
            pool.wait_ge(S("h2_out"), 16 * NT_X)
            pool.wait_ge(S("xg0"), 1)

            def gather(n, s):
                w(pool, "idx", n + 1)
                w(pool, "xt_mm", 2 * (n - 2))
                pool.sem_inc(S("tick"), 1)
                pool.indirect_dma_start(xg[s], None, h2d, bass.IndirectOffsetOnAxis(ap=idx[s][:, 0:1], axis=0),
                                        bounds_check=T_X - 1, oob_is_err=False).then_inc(S(f"gat{s}"), 16)

            def scatter(n, s):
                w(pool, "y", n + 1)
                w(pool, "yy", n + 1)
                pool.sem_inc(S("tick"), 1)
                pool.indirect_dma_start(yd, bass.IndirectOffsetOnAxis(ap=sidx[s], axis=0), yb[s], None,
                                        bounds_check=T_X * TOP_K - 1, oob_is_err=False).then_inc(S(f"ys{s}"), 16)

            def body(i):
                for s in range(ITEM_RING):
                    n = i * ITEM_RING + s
                    if not (isinstance(n, int) and n == 0):
                        scatter(n - 1, (s - 1) % ITEM_RING)
                    gather(n + 2, (s + 2) % ITEM_RING)
            gather(0, 0)
            gather(1, 1)
            n = groups(pool, body)
            scatter(n * ITEM_RING - 1, ITEM_RING - 1)
            for s in range(ITEM_RING):
                pool.wait_ge(S(f"ys{s}"), 16 * n)
            pool.sem_inc(S("scattered"), 1)


        with nc.Block() as block:
            @block.sync
            def _(sp):
                load_moe(sp)

            @block.tensor
            def _(pe):
                moe_pe(pe)

            @block.scalar
            def _(act):
                moe_act(act)

            @block.vector
            def _(dve):
                moe_dve(dve)

            @block.gpsimd
            def _(pool):
                moe_pool(pool)

        end_phase()

        RING2 = 3
        ring2 = [at(WCH * i, WCH) for i in range(RING2)]
        xnT = at(12288, KD * T_X).rearrange("p (k t) -> p k t", k=KD)
        cvT = at(16384, KD * T_X).rearrange("p (k t) -> p k t", k=KD)
        xs = at(31780, NT_X * D).rearrange("p (t d) -> p t d", t=NT_X)
        tables_of = [at(o_, 4096).rearrange("p (f s t) -> p f s t", f=2, s=4) for o_ in (20480, 31780)]
        ssm_w = [at(o_, 2048).rearrange("p (s m c) -> p s m c", s=4, m=4) for o_ in (24576, 35876)]
        merged = at(35876, KD * T_X).rearrange("p (k t) -> p k t", k=KD)
        z = at(39972, 2048).rearrange("p (q t) -> p q t", q=4)
        u_s = at(42020, 2048).rearrange("p (q t) -> p q t", q=4)
        DB = TB + N_COLS2
        rotated = [at(DB + 512 * i, 512) for i in range(4)]
        scanned = [at(DB + 2048 + 512 * i, 512) for i in range(2)]
        cvp = [at(DB + 3072 + 514 * i, 514) for i in range(2)]
        cg = [at(DB + 4100 + 512 * i, 512) for i in range(2)]
        state_in = [[at(37924 + 512 * i, 512) for i in range(2)], [at(38948 + 512 * i, 512) for i in range(2)]]
        pool_tmp = [at(26624, 512), at(27136, 512)]
        gates = [at(DB + 512 * i, 512) for i in range(3)]
        hcol = at(44697, 2432)
        hs_at = [0]

        def tk(n):
            hs_at[0] += n
            assert hs_at[0] <= 2432
            return hcol[:, hs_at[0] - n:hs_at[0]]
        c16 = {nm: tk(16) for nm in ("dt", "mag", "th", "r", "sn", "sh", "cs", "qre", "qim", "nqre", "nqim", "er", "ei", "den", "a", "b", "c", "d")}
        c16i = tk(16).bitcast(I32)
        pw = [(tk(16), tk(16)) for _ in range(9)]
        ssA, rtA, rsA, ssB, rtB, rsB, ssC, rtC, rsC, ssE, rtE, rsE = [tk(4) for _ in range(12)]
        eps2 = tk(1)
        zero1 = tk(1)
        ctmp = [tk(128), tk(128)]
        growf = tk(D)
        sqt = [at(DB + D * i, D) for i in range(2)]
        hidden = [at(16384 + 512 * i, 512) for i in range(22)] + [at(31780 + 4096 + 512 * i, 512) for i in range(10)]
        CHUNKS2 = [("u", 0)] + [("t", j) for j in range(8)] + [("j", j) for j in range(8)] + [("o", 0), ("o", 1)] + \
              [("f1", j) for j in range(8)] + [("f2", j) for j in range(8)]
        FIRST = {}
        for n, (kind, _) in enumerate(CHUNKS2):
            FIRST.setdefault(kind, n)
        WIDTH = dict(u=4096, t=3072, j=4096, o=4096, f1=4096, f2=4096)

        with nc.Block() as block:
            @block.sync
            def _(sp):
                def chunk(n):
                    if n >= RING2:
                        sp.wait_ge(S("used"), n - RING2 + 1)
                    kind, j = CHUNKS2[n]
                    sp.dma_start(ring2[n % RING2][:, 0:WIDTH[kind]], a["w2" + kind][j]).then_inc(S(f"c{n % RING2}_in"), 16)

                def ssm(q):
                    if q >= 2:
                        sp.wait_ge(S("c_mm"), 4 * (q - 1))
                    sp.dma_start(ssm_w[q % 2].rearrange("p s m c -> p (s m c)"), a["ssmw"][q]).then_inc(S(f"sw{q % 2}_in"), 16)
                r0 = ROWS["g_final"][0]
                sp.dma_start(growf, a["rows"][r0:r0 + D].partition_broadcast(P)).then_inc(S("gf_in"), 16)
                chunk(0)
                ssm(0)
                ssm(1)
                for n in range(1, len(CHUNKS2)):
                    chunk(n)
                    kind, j = CHUNKS2[n]
                    if kind == "t" and j in (5, 7):
                        ssm(2 if j == 5 else 3)
                    if kind == "t" and j == 0:
                        sp.wait_ge(S("xmid2"), NT_X)
                        r1 = ROWS["g_final2"][0]
                        sp.dma_start(growf, a["rows"][r1:r1 + D].partition_broadcast(P)).then_inc(S("gf2_in"), 16)
                for t in range(NT_X):
                    sp.wait_ge(S("final"), t + 1)
                    sp.dma_start(out[t * P:(t + 1) * P, :], xr[:, t, :]).then_inc(S("out"), 16)
                sp.wait_ge(S("out"), 16 * NT_X)

            @block.tensor
            def _(pe):
                def arrived(n):
                    pe.wait_ge(S(f"c{n % RING2}_in"), 16 * (n // RING2 + 1))
                    return ring2[n % RING2]

                def transposes(ready, name):
                    for k in range(KD):
                        if k == 0:
                            pe.wait_ge(S(ready), NT_X)
                        if k >= 4:
                            pe.wait_ge(S(name), k - 3)
                        for t in range(NT_X):
                            mm = pe.transpose(bank[k % 4][:, t * P:(t + 1) * P], xs[:, t, k * P:(k + 1) * P], ident)
                        mm.then_inc(S(name + "_mm"), 1)
                    pe.wait_ge(S(name), KD)

                def product(bk, wv, rhs, nk):
                    for k in range(nk):
                        mm = pe.matmul(bk, wv[:, k, :], rhs[:, k, :], start=(k == 0), stop=(k == nk - 1))
                    return mm

                def kv(ap, nk):
                    return ap.rearrange("p (k c) -> p k c", k=nk)
                transposes("xs1", "xn1")
                w = kv(arrived(0), KD)
                for m in range(4):
                    mm = product(bank[4 + m][:, :], w[:, :, m * P:(m + 1) * P], xnT, KD)
                    mm.then_inc(S("u_mm"), 1)
                pe.wait_ge(S("u_mm"), 4)
                pe.sem_inc(S("used"), 1)

                def drive(T):
                    q, s = T // 4, T % 4
                    if T == 0:
                        pe.wait_ge(S("u"), 4)
                    if s == 0:
                        pe.wait_ge(S(f"sw{q % 2}_in"), 16 * (q // 2 + 1))
                    if T >= 2:
                        pe.wait_ge(S("bu_rd"), T - 1)
                    b = 3 + 2 * (T % 2)
                    pe.matmul(bank[b][:, :], ssm_w[q % 2][:, s, 0, :], u_s[:, q, :], start=True, stop=True)
                    pe.matmul(bank[b + 1][:, :], ssm_w[q % 2][:, s, 1, :], u_s[:, q, :], start=True, stop=True).then_inc(S("bu_mm"), 1)

                def read(T):
                    q, s = T // 4, T % 4
                    pe.wait_ge(S("st"), T + 1)
                    pe.wait_ge(S("st_im"), T + 1)
                    pe.wait_ge(S("cq"), T + 1)
                    if s == 0 and q >= 1:
                        pe.wait_ge(S("yt"), q)
                    pe.matmul(bank[7][:, :], ssm_w[q % 2][:, s, 2, :], state_in[T % 2][0], start=(s == 0), stop=False)
                    pe.matmul(bank[7][:, :], ssm_w[q % 2][:, s, 3, :], state_in[T % 2][1], start=False, stop=(s == 3)).then_inc(S("c_mm"), 1)
                for j in range(8):
                    w = arrived(FIRST["t"] + j)[:, 0:3072].rearrange("p (m k c) -> p m k c", m=3, k=KD)
                    drive(2 * j)
                    drive(2 * j + 1)
                    if j >= 1:
                        pe.wait_ge(S("cg"), j)
                    product(bank[0][:, :], w[:, 0], xnT, KD).then_inc(S("tri_mm"), 1)
                    if j >= 1:
                        pe.wait_ge(S("cv"), j)
                    product(bank[1][:, :], w[:, 1], xnT, KD).then_inc(S("tri_mm"), 1)
                    if j >= 1:
                        read(2 * j - 2)
                        read(2 * j - 1)
                        pe.wait_ge(S("yb"), j)
                    product(bank[2][:, :], w[:, 2], xnT, KD).then_inc(S("tri_mm"), 1)
                    pe.wait_ge(S("tri_mm"), 3 * (j + 1))
                    pe.sem_inc(S("used"), 1)
                for j in range(8):
                    c = arrived(FIRST["j"] + j)
                    if j == 0:
                        pe.wait_ge(S("cg"), 8)
                    else:
                        pe.wait_ge(S("sgs"), j)
                    product(bank[0][:, :], kv(c[:, 0:1024], KD), xnT, KD).then_inc(S("jm"), 1)
                    if j == 0:
                        pe.wait_ge(S("cv"), 8)
                    else:
                        pe.wait_ge(S("sgc"), j)
                    product(bank[1][:, :], kv(c[:, 1024:2048], KD), xnT, KD).then_inc(S("jm"), 1)
                    if j == 0:
                        pe.wait_ge(S("yb"), 8)
                    else:
                        pe.wait_ge(S("co"), j)
                    product(bank[2][:, :], kv(c[:, 2048:3072], KD), cvT, KD).then_inc(S("jm"), 1)
                    if j == 0:
                        read(14)
                        read(15)
                        pe.wait_ge(S("z"), 4)
                        pe.wait_ge(S("bu_rd"), 16)
                    else:
                        pe.wait_ge(S("sgb"), j)
                    product(bank[4][:, :], kv(c[:, 3584:4096], 4), z, 4).then_inc(S("jm"), 1)
                    if j >= 1:
                        pe.wait_ge(S("ga"), j)
                    product(bank[3][:, :], kv(c[:, 3072:3584], 4), z, 4).then_inc(S("jm"), 1)
                    pe.wait_ge(S("jm"), 5 * (j + 1))
                    pe.sem_inc(S("used"), 1)
                pe.wait_ge(S("mg"), 8)
                wo = [kv(arrived(FIRST["o"] + h), KD) for h in range(2)]
                for u in range(8):
                    t, h = u // 2, u % 2
                    for k in range(KD):
                        mm = pe.matmul(bank[u][:, :], merged[:, k, t * P:(t + 1) * P], wo[h][:, k, :], start=(k == 0), stop=(k == KD - 1))
                    mm.then_inc(S("o_mm"), 1)
                pe.wait_ge(S("o_mm"), 8)
                pe.sem_inc(S("used"), 2)
                pe.wait_ge(S("r1"), 8)
                transposes("xs2", "xn2")
                for c in range(8):
                    w = kv(arrived(FIRST["f1"] + c), KD)
                    for m in range(4):
                        f = 4 * c + m
                        if f >= 8:
                            pe.wait_ge(S("relu"), f - 7)
                        product(bank[f % 8][:, :], w[:, :, m * P:(m + 1) * P], xnT, KD).then_inc(S("f1_mm"), 1)
                    pe.wait_ge(S("f1_mm"), 4 * (c + 1))
                    pe.sem_inc(S("used"), 1)
                pe.wait_ge(S("rl"), 32)
                for c in range(8):
                    w = arrived(FIRST["f2"] + c).rearrange("p (k c) -> p k c", k=4)
                    for k in range(4):
                        f = 4 * c + k
                        for u in range(8):
                            t, h = u // 2, u % 2
                            mm = pe.matmul(bank[u][:, :], hidden[f][:, t * P:(t + 1) * P], w[:, k, 512 * h:512 * h + 512],
                                           start=(f == 0), stop=(f == 31))
                            if f == 31:
                                mm.then_inc(S("f2_mm"), 1)
                    if c < 7:
                        mm.then_inc(S("f2_c"), 1)
                        pe.wait_ge(S("f2_c"), c + 1)
                        pe.sem_inc(S("used"), 1)

            @block.scalar
            def _(act):
                def squares(ssx, rtx, name, ready):
                    for t in range(NT_X):
                        if ready:
                            act.wait_ge(S(ready[0]), ready[1] * (t + 1))
                        if t >= 2:
                            act.wait_ge(S(name + "_ss"), t - 1)
                        act.activation(sqt[t % 2], xr[:, t, :], ACT.Square, accum_out=ssx[:, t:t + 1]).then_inc(S(name + "_ss"), 1)
                    act.wait_ge(S(name + "_ss"), NT_X)
                    act.activation(rtx, ssx, ACT.Sqrt, scale=1.0 / D, bias=eps2).then_inc(S(name + "_rt"), 1)

                def evac(name, g):
                    for k in range(KD):
                        act.wait_ge(S(name + "_mm"), k + 1)
                        act.activation(xnT[:, k, :], bank[k % 4][:, :], ACT.Copy, scale=col2(g, k)).then_inc(S(name), 1)
                act.wait_ge(S("eps2"), 1)
                squares(ssA, rtA, "a", None)
                squares(ssB, rtB, "b", ("xmid2", 1))
                act.wait_ge(S("theta"), 1)
                act.activation(c16["sn"], c16["r"], ACT.Sin, bias=zero1)
                act.activation(c16["sh"], c16["r"], ACT.Sin, scale=0.5, bias=zero1).then_inc(S("sin"), 1)
                evac("xn1", "g2")
                for m in range(4):
                    act.wait_ge(S("u_mm"), m + 1)
                    act.activation(u_s[:, m, :], bank[4 + m][:, :], ACT.Identity, bias=col2("b_in2", m)).then_inc(S("u"), 1)

                def gelu(q):
                    act.wait_ge(S("yt"), q + 1)
                    act.activation(z[:, q, :], z[:, q, :], ACT.Gelu_apprx_tanh).then_inc(S("z"), 1)
                for j in range(8):
                    act.wait_ge(S("tri_mm"), 3 * j + 1)
                    if j >= 2:
                        act.wait_ge(S("cv"), j - 1)
                    act.activation(cg[j % 2], bank[0][:, :], ACT.Identity, bias=col2("b_in2", 12 + j)).then_inc(S("cg"), 1)
                    if j in (2, 4, 6):
                        gelu(j // 2 - 1)
                for j in range(8):
                    act.wait_ge(S("jm"), 5 * j + 1)
                    if j == 0:
                        act.wait_ge(S("st_im"), 16)
                    else:
                        act.wait_ge(S("mg"), j)
                    act.activation(gates[0], bank[0][:, :], ACT.Sigmoid, bias=col2("b_in2", 28 + j)).then_inc(S("sgs"), 1)
                    act.wait_ge(S("jm"), 5 * j + 2)
                    act.activation(gates[1], bank[1][:, :], ACT.Sigmoid, bias=col2("b_in2", 36 + j)).then_inc(S("sgc"), 1)
                    if j == 0:
                        gelu(3)
                    act.wait_ge(S("jm"), 5 * j + 4)
                    act.activation(gates[2], bank[4][:, :], ACT.Sigmoid).then_inc(S("sgb"), 1)
                act.wait_ge(S("mg"), 8)
                squares(ssC, rtC, "c", ("r1", 2))
                evac("xn2", "gmlp")
                for f in range(32):
                    act.wait_ge(S("f1_mm"), f + 1)
                    act.activation(hidden[f], bank[f % 8][:, :], ACT.Relu).then_inc(S("relu"), 1)
                squares(ssE, rtE, "e", ("r2", 2))

            @block.vector
            def _(dve):
                count = {}

                def link(ins, signal="dve_link"):
                    count[signal] = count.get(signal, 0) + 1
                    ins.then_inc(S(signal), 1)
                    dve.wait_ge(S(signal), count[signal])
                link(dve.memset(zero1, 0.0))
                dve.memset(eps2, EPS).then_inc(S("eps2"), 1)
                for b in range(2):
                    dve.memset(cvp[b][:, 0:2], 0.0)
                c = c16

                def scaled(rtx, rsx, name, outs, signal):
                    dve.wait_ge(S(name + "_rt"), 1)
                    link(dve.reciprocal(rsx, rtx))
                    for t in range(NT_X):
                        if outs is None:
                            dve.scalar_tensor_tensor(out=xr[:, t, :], in0=xr[:, t, :], scalar=rsx[:, t:t + 1], in1=growf,
                                                     op0=ALU.mult, op1=ALU.mult).then_inc(S(signal), 1)
                        else:
                            dve.tensor_scalar(outs[:, t, :], xr[:, t, :], rsx[:, t:t + 1], None, ALU.mult).then_inc(S(signal), 1)
                dve.wait_ge(S("gf_in"), 16)
                scaled(rtA, rsA, "a", None, "xmid2")
                dve.wait_ge(S("xmid2"), NT_X)
                scaled(rtB, rsB, "b", xs, "xs1")

                def expf(dst, src):
                    n, r, p = c["a"], c["b"], c["c"]
                    link(dve.tensor_scalar(n, src, -100.0, 88.0, ALU.max, ALU.min))
                    link(dve.tensor_scalar(r, n, 1.4426950408889634, 12582912.0, ALU.mult, ALU.add))
                    link(dve.tensor_scalar(r, r, -12582912.0, None, ALU.add))
                    link(dve.tensor_scalar(p, r, -126.0, 127.0, ALU.max, ALU.min))
                    link(dve.tensor_scalar(c16i, p, 127.0, 8388608.0, ALU.add, ALU.mult))
                    link(dve.scalar_tensor_tensor(out=n, in0=r, scalar=-0.693359375, in1=n, op0=ALU.mult, op1=ALU.add))
                    link(dve.scalar_tensor_tensor(out=r, in0=r, scalar=2.12194440e-4, in1=n, op0=ALU.mult, op1=ALU.add))
                    link(dve.tensor_scalar(p, r, 1.0 / 5040, None, ALU.mult))
                    for f in (720, 120, 24, 6, 2, 1):
                        link(dve.scalar_tensor_tensor(out=p, in0=p, scalar=1.0 / f, in1=r, op0=ALU.add, op1=ALU.mult))
                    link(dve.tensor_scalar(n, src, -87.336544, None, ALU.is_ge))
                    link(dve.scalar_tensor_tensor(out=p, in0=p, scalar=1.0, in1=n, op0=ALU.add, op1=ALU.mult))
                    link(dve.tensor_tensor(dst, p, c16i.bitcast(F32), ALU.mult))
                lr, li = col2("lam_re", 0, 16), col2("lam_im", 0, 16)
                expf(c["dt"], col2("log_dt", 0, 16))
                link(dve.tensor_tensor(c["d"], lr, c["dt"], ALU.mult))
                expf(c["mag"], c["d"])
                link(dve.tensor_tensor(c["th"], li, c["dt"], ALU.mult))
                link(dve.tensor_scalar(c["a"], c["th"], 0.15915494309189535, 12582912.0, ALU.mult, ALU.add))
                link(dve.tensor_scalar(c["a"], c["a"], -12582912.0, None, ALU.add))
                link(dve.scalar_tensor_tensor(out=c["r"], in0=c["a"], scalar=-6.28125, in1=c["th"], op0=ALU.mult, op1=ALU.add))
                link(dve.scalar_tensor_tensor(out=c["r"], in0=c["a"], scalar=-PI2_B, in1=c["r"], op0=ALU.mult, op1=ALU.add))
                link(dve.scalar_tensor_tensor(out=c["r"], in0=c["a"], scalar=-PI2_C, in1=c["r"], op0=ALU.mult, op1=ALU.add))
                link(dve.tensor_scalar(c["r"], c["r"], -3.1415925, 3.1415925, ALU.max, ALU.min), "theta")
                link(dve.tensor_tensor(c["den"], lr, lr, ALU.mult))
                link(dve.tensor_tensor(c["b"], li, li, ALU.mult))
                link(dve.tensor_tensor(c["den"], c["den"], c["b"], ALU.add))
                link(dve.reciprocal(c["den"], c["den"]))
                dve.wait_ge(S("sin"), 1)
                link(dve.tensor_tensor(c["cs"], c["sh"], c["sh"], ALU.mult))
                link(dve.tensor_scalar(c["cs"], c["cs"], -2.0, 1.0, ALU.mult, ALU.add))
                dve.tensor_copy(pw[0][0], c["cs"])
                dve.tensor_copy(pw[0][1], c["sn"])
                dve.tensor_tensor(c["ei"], c["mag"], c["sn"], ALU.mult)
                link(dve.tensor_tensor(c["er"], c["mag"], c["cs"], ALU.mult))
                link(dve.tensor_scalar(c["er"], c["er"], -1.0, None, ALU.add))
                for L in range(8):
                    pc, ps = pw[L]
                    nc_, ns = pw[L + 1]
                    dve.tensor_tensor(nc_, pc, pc, ALU.mult)
                    dve.scalar_tensor_tensor(out=ns, in0=pc, scalar=2.0, in1=ps, op0=ALU.mult, op1=ALU.mult)
                    link(dve.tensor_tensor(c["a"], ps, ps, ALU.mult))
                    link(dve.tensor_tensor(nc_, nc_, c["a"], ALU.subtract))
                dve.engine_nop().then_inc(S("powers"), 1)
                dve.tensor_tensor(c["a"], c["er"], lr, ALU.mult)
                dve.tensor_tensor(c["b"], c["ei"], li, ALU.mult)
                dve.tensor_tensor(c["c"], c["ei"], lr, ALU.mult)
                link(dve.tensor_tensor(c["d"], c["er"], li, ALU.mult))
                dve.tensor_tensor(c["qre"], c["a"], c["b"], ALU.add)
                link(dve.tensor_tensor(c["qim"], c["c"], c["d"], ALU.subtract))
                dve.tensor_tensor(c["qre"], c["qre"], c["den"], ALU.mult)
                link(dve.tensor_tensor(c["qim"], c["qim"], c["den"], ALU.mult))
                dve.tensor_scalar(c["nqre"], c["qre"], -1.0, None, ALU.mult)
                link(dve.tensor_scalar(c["nqim"], c["qim"], -1.0, None, ALU.mult))

                def states(T):
                    q, s = T // 4, T % 4
                    W = ssm_w[q % 2][:, s]
                    tb = tables_of[q % 2]
                    k1 = slice(T, T + 1)
                    if s == 0:
                        dve.wait_ge(S(f"sw{q % 2}_in"), 16 * (q // 2 + 1))
                    dve.tensor_scalar(ctmp[0], W[:, 3, :], c["qim"][:, k1], None, ALU.mult)
                    link(dve.tensor_scalar(ctmp[1], W[:, 2, :], c["nqim"][:, k1], None, ALU.mult))
                    dve.scalar_tensor_tensor(out=W[:, 2, :], in0=W[:, 2, :], scalar=c["qre"][:, k1], in1=ctmp[0], op0=ALU.mult, op1=ALU.subtract)
                    link(dve.scalar_tensor_tensor(out=W[:, 3, :], in0=W[:, 3, :], scalar=c["nqre"][:, k1], in1=ctmp[1], op0=ALU.mult, op1=ALU.add), "cq")
                    dve.wait_ge(S("bu_mm"), T + 1)
                    dve.wait_ge(S("tab"), q + 1)
                    b = 3 + 2 * (T % 2)
                    bre, bim = bank[b][:, :], bank[b + 1][:, :]
                    cs_, sn_ = tb[:, 0, s, :], tb[:, 1, s, :]
                    dve.tensor_tensor(rotated[0], cs_, bre, ALU.mult)
                    dve.tensor_tensor(rotated[1], sn_, bim, ALU.mult)
                    dve.tensor_tensor(rotated[2], cs_, bim, ALU.mult)
                    link(dve.tensor_tensor(rotated[3], sn_, bre, ALU.mult), "bu_rd")
                    dve.tensor_tensor(rotated[0], rotated[0], rotated[1], ALU.add)
                    link(dve.tensor_tensor(rotated[2], rotated[2], rotated[3], ALU.subtract))
                    if T >= 1:
                        dve.wait_ge(S("ur"), T)
                    mg = bc(c["mag"][:, k1], [P, 512])
                    dve.tensor_tensor_scan(scanned[0], mg, rotated[0], 0.0, ALU.mult, ALU.add)
                    link(dve.tensor_tensor_scan(scanned[1], mg, rotated[2], 0.0, ALU.mult, ALU.add), "w")
                    if T >= 2:
                        dve.wait_ge(S("c_mm"), T - 1)
                    dve.tensor_tensor(state_in[T % 2][1], cs_, scanned[1], ALU.mult)
                    link(dve.tensor_tensor(rotated[1], sn_, scanned[0], ALU.mult))
                    link(dve.tensor_tensor(state_in[T % 2][1], state_in[T % 2][1], rotated[1], ALU.add), "st_im")

                def skip(q):
                    dve.wait_ge(S("c_mm"), 4 * (q + 1))
                    dve.scalar_tensor_tensor(out=z[:, q, :], in0=u_s[:, q, :], scalar=col2("ssm_d", q), in1=bank[7][:, :], op0=ALU.mult, op1=ALU.add).then_inc(S("yt"), 1)
                for j in range(8):
                    states(2 * j)
                    states(2 * j + 1)
                    dve.wait_ge(S("cg"), j + 1)
                    dve.wait_ge(S("tri_mm"), 3 * j + 2)
                    cp = cvp[j % 2]
                    link(dve.scalar_tensor_tensor(out=cp[:, 2:514], in0=bank[1][:, :], scalar=col2("b_in2", 20 + j), in1=cg[j % 2], op0=ALU.add, op1=ALU.mult), "cv")
                    link(dve.tensor_scalar(cvT[:, j, :], cp[:, 2:514], col2("conv_w2", 3 * j + 2), col2("conv_b2", j), ALU.mult, ALU.add))
                    for k in (1, 0):
                        link(dve.scalar_tensor_tensor(out=cvT[:, j, :], in0=cp[:, k:k + 512], scalar=col2("conv_w2", 3 * j + k), in1=cvT[:, j, :], op0=ALU.mult, op1=ALU.add))
                    dve.wait_ge(S("tri_mm"), 3 * j + 3)
                    link(dve.scalar_tensor_tensor(out=cvT[:, j, :], in0=bank[2][:, :], scalar=col2("b_in2", 4 + j), in1=cvT[:, j, :], op0=ALU.add, op1=ALU.mult), "yb")
                    if j in (2, 4, 6):
                        skip(j // 2 - 1)
                for j in range(8):
                    dve.wait_ge(S("sgc"), j + 1)
                    dve.wait_ge(S("jm"), 5 * j + 3)
                    dve.tensor_tensor(gates[1], gates[1], bank[2][:, :], ALU.mult).then_inc(S("co"), 1)
                    if j == 0:
                        skip(3)
                    dve.wait_ge(S("sgb"), j + 1)
                    dve.wait_ge(S("jm"), 5 * j + 5)
                    link(dve.tensor_tensor(gates[2], gates[2], bank[3][:, :], ALU.mult), "ga")
                    link(dve.tensor_tensor(gates[2], gates[2], gates[0], ALU.mult))
                    link(dve.tensor_tensor(merged[:, j, :], gates[2], gates[1], ALU.add), "mg")
                for u in range(8):
                    t, h = u // 2, u % 2
                    dve.wait_ge(S("o_mm"), u + 1)
                    dve.tensor_tensor(xr[:, t, 512 * h:512 * h + 512], xr[:, t, 512 * h:512 * h + 512], bank[u][:, :], ALU.add).then_inc(S("r1"), 1)
                scaled(rtC, rsC, "c", xs, "xs2")
                for f in range(32):
                    dve.wait_ge(S("relu"), f + 1)
                    dve.tensor_tensor(hidden[f], hidden[f], hidden[f], ALU.mult).then_inc(S("rl"), 1)
                dve.wait_ge(S("r1"), 8)
                for u in range(8):
                    t, h = u // 2, u % 2
                    dve.wait_ge(S("f2_mm"), u + 1)
                    dve.tensor_tensor(xr[:, t, 512 * h:512 * h + 512], xr[:, t, 512 * h:512 * h + 512], bank[u][:, :], ALU.add).then_inc(S("r2"), 1)
                dve.wait_ge(S("gf2_in"), 16)
                dve.wait_ge(S("r2"), 8)
                scaled(rtE, rsE, "e", None, "final")

            @block.gpsimd
            def _(pool):
                links = [0]

                def link(ins):
                    links[0] += 1
                    ins.then_inc(S("pool_link"), 1)
                    pool.wait_ge(S("pool_link"), links[0])

                def tables(q, part):
                    tb = tables_of[q % 2]
                    if part == 0:
                        if q >= 2:
                            pool.wait_ge(S("st_im"), 4 * (q - 1))
                            pool.wait_ge(S("st"), 4 * (q - 1))
                        elif q == 1:
                            pool.wait_ge(S("xn1_mm"), KD)
                        pool.memset(tb[:, 0, :, 0:1], 1.0)
                        link(pool.memset(tb[:, 1, :, 0:1], 0.0))
                    for L in (range(7), (7,), (8,), (8,))[part]:
                        n = 1 << L
                        c0, s0 = tb[:, 0, :, 0:n], tb[:, 1, :, 0:n]
                        c1, s1 = tb[:, 0, :, n:2 * n], tb[:, 1, :, n:2 * n]
                        pc, ps = [bc(v[:, 4 * q:4 * q + 4].rearrange("p (s o) -> p s o", o=1), [P, 4, n]) for v in pw[L]]
                        if L < 8:
                            g, t1, t2 = slice(0, 4), tb[:, 0, :, 2 * n:3 * n], tb[:, 1, :, 2 * n:3 * n]
                        else:
                            g = slice(2 * (part - 2), 2 * (part - 2) + 2)
                            t1, t2 = [v.rearrange("p (s t) -> p s t", s=2) for v in pool_tmp]
                        pool.tensor_tensor(c1[:, g], c0[:, g], pc[:, g], ALU.mult)
                        pool.tensor_tensor(s1[:, g], s0[:, g], pc[:, g], ALU.mult)
                        pool.tensor_tensor(t1, s0[:, g], ps[:, g], ALU.mult)
                        link(pool.tensor_tensor(t2, c0[:, g], ps[:, g], ALU.mult))
                        pool.tensor_tensor(c1[:, g], c1[:, g], t1, ALU.subtract)
                        link(pool.tensor_tensor(s1[:, g], s1[:, g], t2, ALU.add))
                    if part == 3:
                        pool.sem_inc(S("tab"), 1)

                def unrotate(T):
                    q, s = T // 4, T % 4
                    tb = tables_of[q % 2]
                    cs_, sn_ = tb[:, 0, s, :], tb[:, 1, s, :]
                    pb = state_in[T % 2]
                    pool.wait_ge(S("w"), T + 1)
                    if T >= 2:
                        pool.wait_ge(S("c_mm"), T - 1)
                    pool.tensor_tensor(pb[0], cs_, scanned[0], ALU.mult)
                    pool.tensor_tensor(pool_tmp[0], sn_, scanned[1], ALU.mult).then_inc(S("ur"), 1)
                    pool.wait_ge(S("ur"), T + 1)
                    pool.tensor_tensor(pb[0], pb[0], pool_tmp[0], ALU.subtract).then_inc(S("st"), 1)
                    pool.wait_ge(S("st"), T + 1)
                pool.wait_ge(S("powers"), 1)
                for part in range(4):
                    tables(0, part)
                for T in range(16):
                    unrotate(T)
                    if T < 12:
                        tables(T // 4 + 1, T % 4)


def _chunks(w, width):
    k, n = w.shape
    return w.reshape(k // P, P, n // width, width).transpose(2, 1, 0, 3).reshape(n // width, P, -1)


def _column(v):
    return v.reshape(-1, P).T


def _layout(g):
    import numpy as np
    a = {"x": g["x"][0], "ctx": g["ctx"][0]}
    a["cT"] = np.stack([g["c"][0].reshape(KD, P), g["c_ctx"].reshape(KD, P)], -1).transpose(1, 0, 2).reshape(P, 2 * KD)
    a["wmod"] = _chunks(g["w_mod"][0], 512)
    a["b_mod_row"] = g["b_mod"][0][2 * D:]
    wi = g["w_in"][0]
    qkvz, ba, cf = wi[:, :2048], wi[:, 2048:2064], wi[:, 2064:]
    pairs = np.stack([cf[:, :512].reshape(D, 4, P), cf[:, 512:].reshape(D, 4, P)], 2).reshape(D, D)
    a["win"] = _chunks(np.concatenate([qkvz, pairs], 1), 512)
    a["wout"] = _chunks(g["w_out"][0], 512)
    a["cols"] = np.concatenate([
        _column(g["g_mix"][0]), _column(g["b_mod"][0][:2 * D]), _column(g["dn_norm_g"][0]),
        g["dn_conv_w"][0].reshape(CONV_K, 12, P).transpose(2, 1, 0).reshape(P, -1),
        g["cf_dw_w"][0].reshape(CF_K, 4, P).transpose(2, 1, 0).reshape(P, -1),
        _column(g["cf_dw_b"][0]), _column(g["cf_ln_g"][0]), _column(g["cf_ln_b"][0]),
        ba.reshape(KD, P, 16).transpose(1, 0, 2).reshape(P, -1)], 1)
    a["cols2"] = np.concatenate([
        g["router_w"][0].reshape(KD, P, N_EXP).transpose(1, 0, 2).reshape(P, -1),
        _column(g["norm_mix_g_2"][0]), _column(g["b_in_2"][0]),
        g["conv_w_2"][0].reshape(3, KD, P).transpose(2, 1, 0).reshape(P, -1),
        _column(g["conv_b_2"][0]), _column(g["norm_mlp_g_2"][0]), _column(g["ssm_d_2"][0]),
        _column(g["lam_re_2"][0]), _column(g["lam_im_2"][0]), _column(np.repeat(g["log_dt_2"][0], 64))], 1)
    a["rows"] = np.concatenate([g["dn_a_log"][0].ravel(), g["dn_dt_bias"][0].ravel(), g["router_bias"][0],
                                g["g_ffn"][0], g["g_final"], g["norm_final_g_2"]])

    def experts(gate, up, down):
        e = gate.shape[0]
        gu = np.concatenate([gate.reshape(e, KD, P, F_EXP), up.reshape(e, KD, P, F_EXP)], -1)
        return np.concatenate([gu.transpose(0, 2, 1, 3).reshape(e, P, -1),
                               down.reshape(e, 2, P, D).transpose(0, 2, 1, 3).reshape(e, P, -1)], -1)
    a["wexp"] = experts(g["exp_w_gate"][0], g["exp_w_up"][0], g["exp_w_down"][0])
    a["wsh"] = experts(g["sh_w_gate"], g["sh_w_up"], g["sh_w_down"])[0]

    def tiles(w):
        return _chunks(w, P)
    w2 = g["w_in_2"][0]
    a["w2u"] = _chunks(w2[:, :512], 512)
    a["w2t"] = np.concatenate([tiles(w2[:, 1536:2560]), tiles(w2[:, 2560:3584]), tiles(w2[:, 512:1536])], -1)
    a["w2j"] = np.concatenate([tiles(w2[:, 3584:4608]), tiles(w2[:, 4608:]), tiles(g["w_conv_out_2"][0]),
                               tiles(g["w_glu_a_2"][0]), tiles(g["w_glu_b_2"][0])], -1)
    a["w2o"] = _chunks(g["w_out_2"][0], 512)
    a["w2f1"] = _chunks(g["w_ff1_2"][0], 512)
    a["w2f2"] = g["w_ff2_2"][0].reshape(8, 4, P, D).transpose(0, 2, 1, 3).reshape(8, P, -1)
    blocks = np.zeros((16, P, 4, P), np.float32)
    for group in range(32):
        tile, s0, c0 = group // 2, group % 2 * 64, group % 8 * 16
        for m, (b, c) in enumerate((("ssm_b_re_2", "ssm_c_re_2"), ("ssm_b_im_2", "ssm_c_im_2"))):
            blocks[tile, c0:c0 + 16, m, s0:s0 + 64] = g[b][0, group].T
            blocks[tile, s0:s0 + 64, 2 + m, c0:c0 + 16] = g[c][0, group].T
    a["ssmw"] = blocks.reshape(4, 4, P, 4 * P).transpose(0, 2, 1, 3).reshape(4, P, -1)
    return {name: np.ascontiguousarray(v) for name, v in a.items()}


def kernel(**inputs):
    import numpy as np
    import concourse.bacc as bacc
    from concourse.bass_utils import run_bass_kernel_spmd

    arrays = _layout({name: np.asarray(v) for name, v in inputs.items()})
    nc = bacc.Bacc("TRN2", target_bir_lowering=False, num_devices=1)
    aps = {name: nc.dram_tensor(f"in_{name}", v.shape, mybir.dt.from_np(v.dtype), kind="ExternalInput").ap()
           for name, v in arrays.items()}
    out = nc.dram_tensor("out", (T_X, D), F32, kind="ExternalOutput").ap()
    h2d = nc.dram_tensor("h2_rows", (T_X, D), F32, kind="Internal").ap()
    yd = nc.dram_tensor("expert_rows", (T_X * TOP_K, D), F32, kind="Internal").ap()
    build(nc, aps, out, h2d, yd)
    r = run_bass_kernel_spmd(nc, [{f"in_{name}": v for name, v in arrays.items()}], core_ids=[0])
    return r.results[0]["out"].reshape(1, T_X, D)
```
